# Optimizing a Trainium2 kernel written in Bass

```python
import math
import jax, jax.numpy as jnp
from jax import lax
import numpy as np

D_MODEL = 2048
BATCH = 1
SEQ = 256
DEPTH = 1

N_META = 16
GRID_W = 64
DA_HEADS = 8
DA_HEAD_DIM = 64
DA_V_DIM = 2 * DA_HEAD_DIM
DA_Q_BLOCK = 128
DA_QK_W = DA_HEADS * 2 * DA_HEAD_DIM
DA_V_W = DA_HEADS * DA_V_DIM
NA_HEADS = 16
NA_HEAD_DIM = 64
NA_W = NA_HEADS * NA_HEAD_DIM
NA_WIN_H = 8
NA_WIN_W = 16
IN_SPLITS = (DA_QK_W, DA_QK_W, DA_V_W, NA_W, NA_W, NA_W, D_MODEL, D_MODEL)
IN_COLS = sum(IN_SPLITS)
PEER_HEADS = 8
PEER_N_KEYS = 128
PEER_N_EXPERTS = PEER_N_KEYS * PEER_N_KEYS
PEER_KEY_DIM = 256
PEER_TOPK = 16
PEER_CHUNK = 128
EPS = 1e-6

kernel_name = "hybrid_diffattn_natten_peer_block"

def rms_norm(x, g):
    xf = x.astype(jnp.float32)
    y = xf * lax.rsqrt(jnp.mean(xf * xf, axis=-1, keepdims=True) + EPS)
    return (y * g.astype(jnp.float32)).astype(x.dtype)

def alibi_slopes(n_heads):
    return jnp.asarray(2.0 ** (-8.0 * np.arange(1, n_heads + 1) / n_heads), dtype=jnp.float32)

def diff_attention(q, k, v, lam, slopes):
    B, L, H = q.shape[0], q.shape[1], q.shape[2]
    scale = DA_HEAD_DIM ** -0.5
    kpos = jnp.arange(L, dtype=jnp.float32)

    def attend(q_blk, qpos):
        s = jnp.einsum('bqhcd,bkhcd->bchqk', q_blk, k).astype(jnp.float32) * scale
        bias = -slopes[:, None, None] * jnp.abs(qpos[:, None] - kpos[None, :])[None]
        p = jax.nn.softmax(s + bias, axis=-1)
        a = p[:, 0] - lam * p[:, 1]
        return jnp.einsum('bhqk,bkhe->bqhe', a.astype(v.dtype), v)

    meta_out = attend(q[:, :N_META], jnp.arange(N_META, dtype=jnp.float32))
    n_real = L - N_META
    nb = n_real // DA_Q_BLOCK
    q_real = q[:, N_META:].reshape(B, nb, DA_Q_BLOCK, H, 2, DA_HEAD_DIM).transpose(1, 0, 2, 3, 4, 5)
    qpos_real = (N_META + jnp.arange(n_real, dtype=jnp.float32)).reshape(nb, DA_Q_BLOCK)
    real_out = lax.map(lambda args: attend(args[0], args[1]), (q_real, qpos_real))
    real_out = real_out.transpose(1, 0, 2, 3, 4).reshape(B, n_real, H, DA_V_DIM)
    return jnp.concatenate([meta_out, real_out], axis=1)

def neighbourhood_attention(q, k, v, rpb):
    B, L, H, dh = q.shape
    n_real = L - N_META
    rows = n_real // GRID_W
    kh = min(NA_WIN_H, rows)
    kw = NA_WIN_W
    scale = dh ** -0.5
    qm, km, vm = q[:, :N_META], k[:, :N_META], v[:, :N_META]
    sm = jnp.einsum('bqhd,bmhd->bhqm', qm, km).astype(jnp.float32) * scale
    meta_out = jnp.einsum('bhqm,bmhd->bqhd', jax.nn.softmax(sm, axis=-1).astype(v.dtype), vm)

    qg = q[:, N_META:].reshape(B, rows, GRID_W, H, dh)
    kg = k[:, N_META:].reshape(B, rows, GRID_W, H, dh)
    vg = v[:, N_META:].reshape(B, rows, GRID_W, H, dh)
    cols = jnp.arange(GRID_W)
    col_start = jnp.clip(cols - kw // 2, 0, GRID_W - kw)
    col_idx = col_start[:, None] + jnp.arange(kw)[None, :]
    dc_idx = col_idx - cols[:, None] + (NA_WIN_W - 1)

    def attend_row(args):
        q_row, r = args
        r0 = jnp.clip(r - kh // 2, 0, rows - kh)
        k_rows = lax.dynamic_slice_in_dim(kg, r0, kh, axis=1)
        v_rows = lax.dynamic_slice_in_dim(vg, r0, kh, axis=1)
        k_nb = k_rows[:, :, col_idx]
        v_nb = v_rows[:, :, col_idx]
        s_win = jnp.einsum('bqhd,bjqwhd->bhqjw', q_row, k_nb).astype(jnp.float32) * scale
        dr_idx = r0 + jnp.arange(kh) - r + (NA_WIN_H - 1)
        bias = rpb[:, dr_idx[None, :, None], dc_idx[:, None, :]]
        s_win = s_win + bias.astype(jnp.float32)[None]
        s_meta = jnp.einsum('bqhd,bmhd->bhqm', q_row, km).astype(jnp.float32) * scale
        s = jnp.concatenate([s_win.reshape(B, H, GRID_W, kh * kw), s_meta], axis=-1)
        p = jax.nn.softmax(s, axis=-1).astype(v.dtype)
        p_win = p[..., :kh * kw].reshape(B, H, GRID_W, kh, kw)
        p_meta = p[..., kh * kw:]
        return (jnp.einsum('bhqjw,bjqwhd->bqhd', p_win, v_nb)
                + jnp.einsum('bhqm,bmhd->bqhd', p_meta, vm))

    out = lax.map(attend_row, (qg.transpose(1, 0, 2, 3, 4), jnp.arange(rows)))
    out = out.transpose(1, 0, 2, 3, 4).reshape(B, n_real, H, dh)
    return jnp.concatenate([meta_out, out], axis=1)

def peer_ffn(x, w_query, sub_keys, expert_u, expert_v):
    B, L, D = x.shape
    T = B * L
    n_chunks = -(-T // PEER_CHUNK)
    pad = n_chunks * PEER_CHUNK - T
    xt = jnp.pad(x.reshape(T, D), ((0, pad), (0, 0))).reshape(n_chunks, PEER_CHUNK, D)

    def chunk(xc):
        q = (xc @ w_query).reshape(PEER_CHUNK, PEER_HEADS, 2, PEER_KEY_DIM // 2)
        s = jnp.einsum('chpk,pnk->chpn', q, sub_keys).astype(jnp.float32)
        s1, i1 = lax.top_k(s[:, :, 0], PEER_TOPK)
        s2, i2 = lax.top_k(s[:, :, 1], PEER_TOPK)
        cand = (s1[..., :, None] + s2[..., None, :]).reshape(PEER_CHUNK, PEER_HEADS, PEER_TOPK * PEER_TOPK)
        sc, ci = lax.top_k(cand, PEER_TOPK)
        e = (jnp.take_along_axis(i1, ci // PEER_TOPK, axis=-1) * PEER_N_KEYS
             + jnp.take_along_axis(i2, ci % PEER_TOPK, axis=-1))
        g = jax.nn.softmax(sc, axis=-1)
        u = expert_u[e]
        v = expert_v[e]
        a = jax.nn.gelu(jnp.einsum('cd,chkd->chk', xc, u).astype(jnp.float32))
        return jnp.einsum('chk,chkd->cd', (g * a).astype(xc.dtype), v)

    out = lax.map(chunk, xt).reshape(n_chunks * PEER_CHUNK, D)[:T]
    return out.reshape(B, L, D)

def setup_inputs(seed: int = 0) -> dict:
    key = jax.random.key(seed)
    ks = jax.random.split(key, 24)
    f32 = jnp.float32
    nrm = lambda k, shape, s: jax.random.normal(k, shape, f32) * s
    gain = lambda k, shape: 1.0 + 0.01 * jax.random.normal(k, shape, f32)
    return {
        'x': nrm(ks[0], (BATCH, SEQ, D_MODEL), 1.0),
        'meta_tokens': nrm(ks[1], (N_META, D_MODEL), 1.0),
        'norm1_g': gain(ks[2], (DEPTH, D_MODEL)),
        'w_in': nrm(ks[3], (DEPTH, D_MODEL, IN_COLS), D_MODEL ** -0.5),
        'da_q_norm_g': gain(ks[4], (DEPTH, DA_HEAD_DIM)),
        'da_k_norm_g': gain(ks[5], (DEPTH, DA_HEAD_DIM)),
        'lambda_q1': nrm(ks[6], (DEPTH, DA_HEAD_DIM), 0.1),
        'lambda_k1': nrm(ks[7], (DEPTH, DA_HEAD_DIM), 0.1),
        'lambda_q2': nrm(ks[8], (DEPTH, DA_HEAD_DIM), 0.1),
        'lambda_k2': nrm(ks[9], (DEPTH, DA_HEAD_DIM), 0.1),
        'da_out_norm_g': gain(ks[10], (DEPTH, DA_V_DIM)),
        'na_q_norm_g': gain(ks[11], (DEPTH, NA_HEAD_DIM)),
        'na_k_norm_g': gain(ks[12], (DEPTH, NA_HEAD_DIM)),
        'na_rpb': nrm(ks[13], (DEPTH, NA_HEADS, 2 * NA_WIN_H - 1, 2 * NA_WIN_W - 1), 0.1),
        'w_branch_da': nrm(ks[14], (DEPTH, DA_V_W, D_MODEL), DA_V_W ** -0.5),
        'w_branch_na': nrm(ks[15], (DEPTH, NA_W, D_MODEL), NA_W ** -0.5),
        'w_out': nrm(ks[16], (DEPTH, D_MODEL, D_MODEL), D_MODEL ** -0.5),
        'norm2_g': gain(ks[17], (DEPTH, D_MODEL)),
        'peer_w_query': nrm(ks[18], (DEPTH, D_MODEL, PEER_HEADS * PEER_KEY_DIM), D_MODEL ** -0.5),
        'peer_sub_keys': nrm(ks[19], (DEPTH, 2, PEER_N_KEYS, PEER_KEY_DIM // 2), (PEER_KEY_DIM // 2) ** -0.5),
        'peer_u': nrm(ks[20], (DEPTH, PEER_N_EXPERTS, D_MODEL), D_MODEL ** -0.5),
        'peer_v': nrm(ks[21], (DEPTH, PEER_N_EXPERTS, D_MODEL), 0.5),
    }

def reference(x, meta_tokens, norm1_g, w_in, da_q_norm_g, da_k_norm_g, lambda_q1, lambda_k1,
              lambda_q2, lambda_k2, da_out_norm_g, na_q_norm_g, na_k_norm_g, na_rpb,
              w_branch_da, w_branch_na, w_out, norm2_g, peer_w_query, peer_sub_keys, peer_u, peer_v):
    B, S, D = x.shape
    L = S + N_META
    meta = jnp.broadcast_to(meta_tokens[None].astype(x.dtype), (B, N_META, D))
    h = jnp.concatenate([meta, x], axis=1)
    slopes = alibi_slopes(DA_HEADS)
    split_pts = [int(c) for c in np.cumsum(IN_SPLITS)[:-1]]
    for l in range(DEPTH):
        xn = rms_norm(h, norm1_g[l])
        proj = xn @ w_in[l]
        q_da, k_da, v_da, q_na, k_na, v_na, gate_da, gate_na = jnp.split(proj, split_pts, axis=-1)

        q_da = rms_norm(q_da.reshape(B, L, DA_HEADS, 2, DA_HEAD_DIM), da_q_norm_g[l])
        k_da = rms_norm(k_da.reshape(B, L, DA_HEADS, 2, DA_HEAD_DIM), da_k_norm_g[l])
        v_da = v_da.reshape(B, L, DA_HEADS, DA_V_DIM)
        lam_init = 0.8 - 0.6 * math.exp(-0.3 * l)
        lam = (jnp.exp(jnp.sum(lambda_q1[l].astype(jnp.float32) * lambda_k1[l].astype(jnp.float32)))
               - jnp.exp(jnp.sum(lambda_q2[l].astype(jnp.float32) * lambda_k2[l].astype(jnp.float32)))
               + lam_init)
        o_da = diff_attention(q_da, k_da, v_da, lam, slopes)
        o_da = rms_norm(o_da, da_out_norm_g[l]) * (1.0 - lam_init)
        y_da = o_da.reshape(B, L, DA_V_W) @ w_branch_da[l]

        q_na = rms_norm(q_na.reshape(B, L, NA_HEADS, NA_HEAD_DIM), na_q_norm_g[l])
        k_na = rms_norm(k_na.reshape(B, L, NA_HEADS, NA_HEAD_DIM), na_k_norm_g[l])
        v_na = v_na.reshape(B, L, NA_HEADS, NA_HEAD_DIM)
        o_na = neighbourhood_attention(q_na, k_na, v_na, na_rpb[l])
        y_na = o_na.reshape(B, L, NA_W) @ w_branch_na[l]

        mixed = jax.nn.sigmoid(gate_da) * y_da + jax.nn.sigmoid(gate_na) * y_na
        h = h + mixed @ w_out[l]

        h = h + peer_ffn(rms_norm(h, norm2_g[l]), peer_w_query[l], peer_sub_keys[l], peer_u[l], peer_v[l])
    return h[:, N_META:]


_drawn_inputs = setup_inputs


def setup_inputs(seed=0):
    import zlib

    import numpy as np

    out = dict(_drawn_inputs(seed))
    spreads = {}
    factors = {'da_q_norm_g': 3.941,
     'da_k_norm_g': 3.435,
     'lambda_k2': 4.151,
     'da_out_norm_g': 3.473,
     'na_q_norm_g': 8.0,
     'na_k_norm_g': 8.0}
    for name, (base, spread) in spreads.items():
        noise = np.random.default_rng([zlib.crc32(name.encode()), seed]).standard_normal(out[name].shape)
        drawn = base * np.exp(spread * noise) if base else spread * noise
        out[name] = __import__('jax').numpy.asarray(drawn.astype(out[name].dtype))
    for name, factor in factors.items():
        out[name] = (out[name] * factor).astype(out[name].dtype)
    return out
```

```python
from contextlib import ExitStack

import numpy as np

import concourse.bass as bass
from concourse import mybir

F32 = mybir.dt.float32
F32R = mybir.dt.float32r
U32 = mybir.dt.uint32
ALU = mybir.AluOpType
ACT = mybir.ActivationFunctionType
AX = mybir.AxisListType

P = 128
D = 2048
KC = D // P
T = 256
META = 16
L = T + META
TT = T // P
HEADS = 8
DH = 64
GRID_W = 64
ROWS = T // GRID_W
RPB_H, RPB_W = 15, 31
RPB_PITCH = 128
WIN_W = 16
TOPK = 16
EPS = 1e-6
LAM_INIT = 0.2
MASKED = -1e30
LOWEST = -3.0e38

CH = 1024
RING = 4
RING_A = 5
BLOCKS_A = 10
CHUNKS_A = 2 * BLOCKS_A
BASE_B = HEADS * CHUNKS_A
BASE_C = BASE_B + 2 * KC
BASE_D = BASE_C + 2 * KC
BASE_E = BASE_D + 2 * KC
N_CHUNKS = BASE_E + 4 * P
AHEAD = 3

G1, G2, GQD, GKD, GQN, GKN, GOD = 0, 16, 32, 33, 34, 35, 36
N_GAINS = 37


def block_kernel(nc, h_turned, gains, lambdas, alibi, na_mask, rpb, ident_d, ones_d, pair_ones_d, iota_d,
                 sub_keys, w_in, w_branch, w_out, w_query, peer_u, peer_v, out):
    ctx = ExitStack()
    with ctx:
        def sem(name):
            return ctx.enter_context(nc.semaphore(name))

        cursor = [16512]

        def place(name, shape, dt, at=None):
            size = int(np.prod(shape[1:])) * 4
            if at is None:
                at = cursor[0]
                cursor[0] += -(-size // 32) * 32
            return nc.alloc_sbuf_tensor_at(name, shape, dt, offset=at)

        at_x = cursor[0]
        x_hi = place("x_hi", [P, KC, L], F32R)
        x_lo = place("x_lo", [P, KC, L], F32R)
        chunk_hi, chunk_raw, chunk_lo = [], [], []
        for s in range(RING_A):
            at_p = cursor[0]
            chunk_hi.append(place(f"chunk_hi{s}", [P, CH], F32R))
            at_raw = cursor[0]
            chunk_raw.append(place(f"chunk_raw{s}", [P, CH], F32))
            chunk_lo.append(place(f"chunk_lo{s}", [P, CH], F32R, at=at_raw))
        cursor[0] = at_p + 10240
        iota = place("iota", [P, P], F32)
        at_squares = cursor[0]
        ident = place("ident", [P, P], F32)
        ones = place("ones", [P, P], F32)
        pair_ones = place("pair_ones", [P, P], F32)
        cursor[0] += 512
        gain = place("gain", [P, N_GAINS], F32)
        eps = place("eps", [P, 1], F32)
        neg_lam = place("neg_lam", [P, 1], F32)
        lam_e = place("lam_e", [P, 2], F32)
        stat_max = place("stat_max", [P, 8], F32)
        stat_neg = place("stat_neg", [P, 8], F32)
        stat_sum = place("stat_sum", [P, 8], F32)
        stat_inv = place("stat_inv", [P, 8], F32)
        at_w = cursor[0]
        assert at_w + P * T * 4 <= nc.sbuf_usable_end, (at_w + P * T * 4, nc.sbuf_usable_end)

        w2 = nc.alloc_sbuf_tensor_at("w2", [P, P, T], F32, offset=at_w)
        cursor[0] = at_w
        h_t = place("h_t", [P, KC, L], F32)
        gates = place("gates", [P, 2 * KC, T], F32)
        o_hi = place("o_hi", [P, 2 * HEADS, T], F32R)
        o_lo = place("o_lo", [P, 2 * HEADS, T], F32R)
        at_scratch = cursor[0]
        da_bias = place("da_bias", [P, TT, L], F32)
        na_bias = place("na_bias", [P, 4, L], F32)
        rpb_t = place("rpb_t", [P, 2, 4, T], F32)
        mask = place("mask", [P, T], F32)
        t_da = place("t_da", [P, 4, L], F32)
        t_na = place("t_na", [P, 4, L], F32)
        sq = place("sq", [P, L], F32)
        ln_r = place("ln_r", [P, L], F32)
        rstd = place("rstd", [P, L], F32)
        qk = place("qk", [P, 4, L], F32)
        v_t = place("v_t", [P, L], F32)
        v_tok = place("v_tok", [P, 2, 2, P], F32)
        v_meta = place("v_meta", [META, 2, P], F32)
        p_t = place("p_t", [P, 3, TT, T], F32)
        p_meta = place("p_meta", [META, 3, T], F32)
        o_f = place("o_f", [P, T], F32)
        gate_e = place("gate_e", [P, T], F32)
        assert cursor[0] <= at_w + P * T * 4
        lam_v = nc.alloc_sbuf_tensor_at("lam_v", [P, 4, DH], F32, offset=at_scratch + 2176)
        lam_w = nc.alloc_sbuf_tensor_at("lam_w", [P, DH], F32, offset=at_scratch + 2176 + 1024)
        sq_big = nc.alloc_sbuf_tensor_at("sq_big", [P, KC, L], F32, offset=at_w + 17408)
        xf = nc.alloc_sbuf_tensor_at("xf", [P, KC, L], F32, offset=at_w + 17408 + 17408)
        cursor[0] = at_scratch
        m_hi = place("m_hi", [P, KC, T], F32R)
        m_lo = place("m_lo", [P, KC, T], F32R)
        m_a = place("m_a", [P, 2, T], F32)
        m_b = place("m_b", [P, 2, T], F32)
        m_f = place("m_f", [P, 2, T], F32)
        sq2 = place("sq2", [P, 2, T], F32)
        x2f = nc.alloc_sbuf_tensor_at("x2f", [P, KC, T], F32, offset=at_w + 17408)
        ln_r2 = place("ln_r2", [P, T], F32)
        rstd2 = place("rstd2", [P, T], F32)
        cursor[0] = at_w + 17408 + 32768
        subk = place("subk", [P, 2, P], F32)
        q_sb = place("q_sb", [P, 2, T], F32)
        s_sb = place("s_sb", [P, 4, P], F32)
        s_rest = place("s_rest", [P, 4, P], F32)
        top = place("top", [P, 4, TOPK], F32)
        top_i = place("top_i", [P, 4, TOPK], U32)
        top_f = place("top_f", [P, 4, TOPK], F32)
        cand = place("cand", [P, TT, TOPK * TOPK], F32)
        cand_rest = place("cand_rest", [P, TT, TOPK * TOPK], F32)
        best = place("best", [P, TT, TOPK], F32)
        best_i = place("best_i", [P, TT, TOPK], U32)
        pos_i = place("pos_i", [P, TT, 2, TOPK], U32)
        pos_f = place("pos_f", [P, TT, 2, TOPK], F32)
        eq = place("eq", [P, 4, TOPK, TOPK], F32)
        eqv = place("eqv", [P, 4, TOPK, TOPK], F32)
        neg_best = place("neg_best", [P, TT], F32)
        g_e = place("g_e", [P, TT, TOPK], F32)
        g_sum = place("g_sum", [P, TT], F32)
        g_inv = place("g_inv", [P, TT], F32)
        route = place("route", [P, 3, TT, P], F32)
        assert cursor[0] <= at_w + P * T * 4
        route_t = nc.alloc_sbuf_tensor_at("route_t", [P, 3, T], F32, offset=at_p)
        hot1 = nc.alloc_sbuf_tensor_at("hot1", [P, 4, P], F32, offset=at_p + 3072)
        hot2 = nc.alloc_sbuf_tensor_at("hot2", [P, 4, P], F32, offset=at_squares)
        p_hi = nc.alloc_sbuf_tensor_at("p_hi", [P, 2, T], F32R, offset=at_p)
        p_lo = nc.alloc_sbuf_tensor_at("p_lo", [P, 2, T], F32R, offset=at_p + 2048)
        gelu = nc.alloc_sbuf_tensor_at("gelu", [P, T], F32, offset=at_p + 4096)
        p_f = nc.alloc_sbuf_tensor_at("p_f", [P, T], F32, offset=at_p + 5120)
        acc = nc.alloc_sbuf_tensor_at("acc", [P, 2, 512], F32, offset=at_p + 6144)
        out_sb = nc.alloc_sbuf_tensor_at("out_sb", [P, 6, 512], F32, offset=at_w)

        bank = [ctx.enter_context(nc.psum_tensor(f"bank{i}", [P, 512], F32)) for i in range(8)]
        blk = [bank[0], bank[1]]
        ms = bank[2]
        sc = [bank[3], bank[4]]
        turn, turn_m, att = bank[5], bank[6], bank[7]
        held = bank[0:6]
        up, spare = bank[6], bank[7]

        landed = [sem(f"landed{s}") for s in range(RING_A)]
        hi_ready = sem("hi_ready")
        lo_ready = sem("lo_ready")
        chunk_used = sem("chunk_used")
        h_in, const_in, lam_in, rpb_in = sem("h_in"), sem("const_in"), sem("lam_in"), [sem("rpb_in0"), sem("rpb_in1")]
        subk_in = sem("subk_in")
        consts_set = sem("consts_set")
        lam_dots, lam_exp, lam_done, lam_step = sem("lam_dots"), sem("lam_exp"), sem("lam_done"), sem("lam_step")
        sq_ready, ms_ready, ln_ready = sem("sq_ready"), sem("ms_ready"), sem("ln_ready")
        r_ready, normed = sem("r_ready"), sem("normed")
        xf_ready, x_hi_ready, x_lo_ready = sem("xf_ready"), sem("x_hi_ready"), sem("x_lo_ready")
        vt_ready, v_turned, v_ready = sem("vt_ready"), sem("v_turned"), sem("v_ready")
        s_ready, max_ready, t_ready = sem("s_ready"), sem("max_ready"), sem("t_ready")
        p_ready, inv_ready, mix_half, p_normed = sem("p_ready"), sem("inv_ready"), sem("mix_half"), sem("p_normed")
        p_turned, pt_ready, pv_done = sem("p_turned"), sem("pt_ready"), sem("pv_done")
        na_bias_ready, da_bias_ready = sem("na_bias_ready"), sem("da_bias_ready")
        o_hi_ready, o_lo_ready = sem("o_hi_ready"), sem("o_lo_ready")
        gate_exp, gate_den, gate_ready = sem("gate_exp"), sem("gate_den"), sem("gate_ready")
        m_parts, m_ready, m_hi_ready, m_lo_ready = sem("m_parts"), sem("m_ready"), sem("m_hi_ready"), sem("m_lo_ready")
        h2_ready, sq2_ready, sq2_used = sem("h2_ready"), sem("sq2_ready"), sem("sq2_used")
        q_ready, ps_ready, ssb_ready = sem("q_ready"), sem("ps_ready"), sem("ssb_ready")
        top_step, best_step, decode_step = sem("top_step"), sem("best_step"), sem("decode_step")
        neg_ready, g_exp_ready, g_inv_ready, routed = sem("neg_ready"), sem("g_exp_ready"), sem("g_inv_ready"), sem("routed")
        route_turned, route_ready = sem("route_turned"), sem("route_ready")
        seeded, acc_ready = sem("seeded"), sem("acc_ready")
        hot_ready, table_done, table_ready = sem("hot_ready"), sem("table_done"), sem("table_ready")
        gelu_ready, pf_ready = sem("gelu_ready"), sem("pf_ready")
        p_hi_ready, p_lo_ready = sem("p_hi_ready"), sem("p_lo_ready")
        spare_done, spare_added = sem("spare_done"), sem("spare_added")
        out_ready, stored = sem("out_ready"), sem("stored")

        def load_chunk_a(sp, h, j, src, first=False):
            if not first:
                sp.wait_ge(chunk_used, CHUNKS_A * h + j - RING_A + 1)
            sp.dma_start(chunk_raw[j % RING_A][:], src).then_inc(landed[j % RING_A], 16)

        def load_chunk(sp, quad, slot, src):
            sp.wait_ge(chunk_used, 4 * quad + slot - RING + 1)
            sp.dma_start(chunk_raw[slot][:], src).then_inc(landed[slot], 16)

        def wait_alone(eng, semaphore, value):
            eng.wait_ge(semaphore, value)
            eng.nop(nofuse=True)

        def split_hi_a(act, h, j):
            act.wait_ge(landed[j % RING_A], 16 * (CHUNKS_A // RING_A * h + j // RING_A + 1))
            act.activation(chunk_hi[j % RING_A][:], chunk_raw[j % RING_A][:], ACT.Copy).then_inc(hi_ready, 1)

        def split_hi(act, quad, slot):
            act.wait_ge(landed[slot], 16 * (quad + 1 - BASE_B // RING + BASE_B // RING_A))
            act.activation(chunk_hi[slot][:], chunk_raw[slot][:], ACT.Copy).then_inc(hi_ready, 1)

        def split_lo_at(dve, number, slot):
            dve.wait_ge(hi_ready, number + 1)
            dve.tensor_tensor(chunk_lo[slot][:], chunk_raw[slot][:], chunk_hi[slot][:].bitcast(F32),
                              ALU.subtract).then_inc(lo_ready, 1)

        def split_lo(dve, quad, slot):
            split_lo_at(dve, 4 * quad + slot, slot)

        def step(split, eng, quad, j):
            split(eng, quad + (j + AHEAD) // RING, (j + AHEAD) % RING)

        def products(pe, number, slot, outp, rhs_hi, rhs_lo, kc0, n, start, stop):
            pe.wait_ge(lo_ready, number + 1)
            for k in range(8):
                w_hi = chunk_hi[slot][:, k * P:(k + 1) * P]
                w_lo = chunk_lo[slot][:, k * P:(k + 1) * P]
                r_hi, r_lo = rhs_hi[:, kc0 + k, 0:n], rhs_lo[:, kc0 + k, 0:n]
                pe.matmul(outp, w_hi, r_lo, start=start and k == 0, stop=False)
                pe.matmul(outp, w_lo, r_hi, start=False, stop=False)
                last = pe.matmul(outp, w_hi, r_hi, start=False, stop=stop and k == 7)
            last.then_inc(chunk_used, 1)

        NORMS = 5
        NORM_BLOCK = {0: 0, 1: 1, 2: 3, 3: 4}
        NORM_COLS = (T, L, T, L, T)
        block = ctx.enter_context(nc.Block())

        @block.sync
        def _(sp):
            for g in range(4):
                sp.dma_start(h_t[:, 4 * g:4 * g + 4, :], h_turned[:, 4 * g:4 * g + 4, :]).then_inc(h_in, 16)
                if g == 0:
                    for dst, src in ((ident, ident_d), (iota, iota_d), (ones, ones_d), (pair_ones, pair_ones_d),
                                     (gain, gains), (mask, na_mask), (da_bias, alibi)):
                        sp.dma_start(dst[:], src).then_inc(const_in, 16)
                    sp.dma_start(lam_v[:], lambdas).then_inc(lam_in, 16)
            for j in range(CHUNKS_A):
                load_chunk_a(sp, 0, j, w_in[j], first=j < RING_A)
            with sp.Fori(1, HEADS) as h:
                for j in range(CHUNKS_A):
                    load_chunk_a(sp, h, j, w_in[CHUNKS_A * h + j])
            for base, src in ((BASE_B, w_branch), (BASE_C, w_out), (BASE_D, w_query)):
                with sp.Fori(0, HEADS) as i:
                    for j in range(4):
                        load_chunk(sp, base // 4 + i, j, src[4 * i + j])
                if base == BASE_C:
                    sp.wait_ge(chunk_used, BASE_C)
                    sp.dma_start(subk[:], sub_keys).then_inc(subk_in, 16)
            for j in range(2):
                load_chunk(sp, BASE_E // 4, j, peer_u[j])
            with sp.Fori(1, P) as b:
                for j in range(2):
                    load_chunk(sp, BASE_E // 4 - 1 + b, 2 + j, peer_u[2 * b + j])
                for j in range(2):
                    load_chunk(sp, BASE_E // 4 + b, j, peer_v[b - 1, j])
            for j in range(2):
                load_chunk(sp, N_CHUNKS // 4 - 1, 2 + j, peer_v[P - 1, j])
            for k in range(8):
                if k < 6:
                    sp.wait_ge(out_ready, k + 1)
                else:
                    sp.wait_ge(spare_added, 2 * P)
                src = out_sb[:, k, :] if k < 6 else acc[:, k - 6, :]
                sp.dma_start(out[(k // 4) * P:(k // 4 + 1) * P, (k % 4) * 512:(k % 4 + 1) * 512],
                             src).then_inc(stored, 16)
            sp.wait_ge(stored, 8 * 16)

        @block.gpsimd
        def _(pool):
            def load_rpb(h, par):
                for hh in range(2):
                    for tt in range(TT):
                        for half in range(2):
                            r = 2 * tt + half
                            src = skewed(rpb[h, hh, 7 - r, 0, GRID_W - 1:GRID_W])
                            pool.dma_start(rpb_t[half * GRID_W:(half + 1) * GRID_W, par, 2 * tt + hh, :]
                                           .rearrange("p (a b) -> p a b", a=ROWS), src).then_inc(rpb_in[par], 16)

            def skewed(first):
                return bass.AP(tensor=first.tensor, offset=first.offset,
                               ap=[[RPB_PITCH - 1, GRID_W], [GRID_W * RPB_PITCH, ROWS], [1, GRID_W]])

            def bias(h, par, rounds):
                pool.wait_ge(rpb_in[par], 128 * rounds)
                for u in range(4):
                    pool.tensor_tensor(na_bias[:, u, 0:T], rpb_t[:, par, u, :], mask[:], ALU.add) \
                        .then_inc(na_bias_ready, 1)

            load_rpb(0, 0)
            load_rpb(1, 1)
            pool.wait_ge(lam_dots, 2)
            pool.wait_ge(const_in, 7 * 16)
            pool.memset(na_bias[:, :, T:L], 0.0).then_inc(na_bias_ready, 1)
            bias(0, 0, 1)
            pool.wait_ge(max_ready, 4)
            pool.tensor_scalar(da_bias[:], da_bias[:], 0.5, None, ALU.mult).then_inc(da_bias_ready, 1)

            def rest(h, par, rounds, more):
                pool.wait_ge(max_ready, 8 * h)
                bias(h, par, rounds)
                if not more:
                    return
                load_rpb(h + 1, 1 - par)
                wait_alone(pool, max_ready, 8 * h + 4)
                pool.tensor_scalar(da_bias[:], da_bias[:], 0.5, None, ALU.mult).then_inc(da_bias_ready, 1)

            with pool.Fori(0, 3) as i:
                rest(2 * i + 1, 1, i + 1, True)
                rest(2 * i + 2, 0, i + 2, True)
            rest(HEADS - 1, 1, 4, False)

        @block.scalar
        def _(act):
            act.preload_act_table_set("natural_log_exp_and_others")
            for g in range(4):
                if g == 0:
                    act.wait_ge(h_in, 4 * 16)
                act.activation(sq_big[:, 4 * g:4 * g + 4, :], h_t[:, 4 * g:4 * g + 4, :], ACT.Square) \
                    .then_inc(sq_ready, 1)
            act.wait_ge(lam_dots, 2)
            act.activation(lam_e[:], lam_e[:], ACT.Exp).then_inc(lam_exp, 1)
            act.wait_ge(consts_set, 1)
            act.wait_ge(ms_ready, 1)
            act.activation(ln_r[:], ms[:, 0:L], ACT.Ln, scale=1.0 / D, bias=eps[:]).then_inc(ln_ready, 1)
            act.wait_ge(ln_ready, 1)
            act.activation(rstd[:], ln_r[:], ACT.Exp, scale=-0.5).then_inc(r_ready, 1)
            for j in range(AHEAD):
                split_hi_a(act, 0, j)
            for g in range(4):
                act.wait_ge(xf_ready, g + 1)
                act.activation(x_hi[:, 4 * g:4 * g + 4, :], xf[:, 4 * g:4 * g + 4, :], ACT.Copy).then_inc(x_hi_ready, 1)

            def head(h, first):
                def square(i):
                    n = NORM_COLS[i]
                    src = att if i == 4 else blk[NORM_BLOCK[i] % 2]
                    if i == 4:
                        act.wait_ge(pv_done, 3 * h + 1)
                    else:
                        act.wait_ge(chunk_used, CHUNKS_A * h + 2 * NORM_BLOCK[i] + 2)
                    act.activation(sq[:, 0:n], src[:, 0:n], ACT.Square).then_inc(sq_ready, 1)

                def rsqrt(i, width):
                    n = NORM_COLS[i]
                    act.wait_ge(ms_ready, NORMS * h + i + 2)
                    act.activation(ln_r[:, 0:n], ms[:, 0:n], ACT.Ln, scale=1.0 / width, bias=eps[:]) \
                        .then_inc(ln_ready, 1)
                    act.wait_ge(ln_ready, NORMS * h + i + 2)
                    if not (first and i == 0):
                        act.wait_ge(normed, NORMS * h + i)
                    act.activation(rstd[:, 0:n], ln_r[:, 0:n], ACT.Exp, scale=-0.5).then_inc(r_ready, 1)

                def copy_v(i):
                    act.wait_ge(chunk_used, CHUNKS_A * h + (6 if i == 0 else 12))
                    if not (first and i == 0):
                        act.wait_ge(v_turned, 2 * h + i)
                    act.activation(v_t[:], blk[0 if i == 0 else 1][:, 0:L], ACT.Copy).then_inc(vt_ready, 1)

                def exp_units(u0):
                    act.wait_ge(t_ready, 4 * h + u0 // 2 + 1)
                    buf = t_da if u0 < 4 else t_na
                    for u in (u0, u0 + 1):
                        act.activation(buf[:, u % 4, :], buf[:, u % 4, :], ACT.Exp, bias=stat_neg[:, u:u + 1],
                                       accum_out=stat_sum[:, u:u + 1]).then_inc(p_ready, 1)

                def gate(k):
                    act.wait_ge(chunk_used, CHUNKS_A * h + 14 + 2 * k)
                    if not (first and k == 0):
                        act.wait_ge(gate_ready, 4 * h + k)
                    act.activation(gate_e[:], blk[k % 2][:, 0:T], ACT.Exp, scale=-1.0).then_inc(gate_exp, 1)

                def copy_turned(i):
                    act.wait_ge(p_turned, 3 * h + i + 1)
                    if not first:
                        act.wait_ge(pv_done, 3 * h - 2 + i)
                    act.activation(p_t[:, i, :, :].rearrange("p a b -> p (a b)"), turn[:], ACT.Copy) \
                        .then_inc(pt_ready, 1)
                    act.activation(p_meta[:, i, :], turn_m[0:META, 0:T], ACT.Copy).then_inc(pt_ready, 1)

                def tick(j):
                    split_hi_a(act, h, j + AHEAD)

                tick(0); tick(1); tick(2); square(0); tick(3); rsqrt(0, DH)
                tick(4); square(1); tick(5); rsqrt(1, DH)
                tick(6); copy_v(0); tick(7); exp_units(0)
                tick(8); exp_units(2); square(2); tick(9); rsqrt(2, DH)
                tick(10); copy_turned(0); square(3); tick(11); rsqrt(3, DH)
                tick(12); copy_v(1); square(4); tick(13); rsqrt(4, P)
                exp_units(4)
                tick(14); gate(0)
                act.wait_ge(normed, NORMS * h + 5)
                act.activation(o_hi[:, h, :], o_f[:], ACT.Copy).then_inc(o_hi_ready, 1)
                tick(15); exp_units(6)
                tick(16); gate(1); copy_turned(1)
                tick(17); copy_turned(2)
                tick(18); gate(2); tick(19)
                act.wait_ge(pv_done, 3 * h + 3)
                act.activation(o_hi[:, HEADS + h, :], att[:, 0:T], ACT.Copy).then_inc(o_hi_ready, 1)
                gate(3)

            head(0, True)
            with act.Fori(1, HEADS) as h:
                head(h, False)

            with act.Fori(0, HEADS) as i:
                for j in range(4):
                    if j % 2 == 1:
                        act.wait_ge(m_ready, 2 * i + j // 2 + 1)
                        act.activation(m_hi[:, 2 * i + j // 2, :], m_f[:, j // 2, :], ACT.Copy).then_inc(m_hi_ready, 1)
                    step(split_hi, act, BASE_B // 4 + i, j)

            def out_rows(i, first):
                for j in range(4):
                    if j % 2 == 1:
                        act.wait_ge(h2_ready, 2 * i + j // 2 + 1)
                        if not first:
                            act.wait_ge(sq2_used, 2 * i + j // 2 - 1)
                        act.activation(sq2[:, j // 2, :], h_t[:, 2 * i + j // 2, 0:T], ACT.Square).then_inc(sq2_ready, 1)
                    step(split_hi, act, BASE_C // 4 + i, j)
            out_rows(0, True)
            with act.Fori(1, HEADS) as i:
                out_rows(i, False)

            act.wait_ge(sq2_used, KC)
            act.activation(ln_r2[:], ms[:, 0:T], ACT.Ln, scale=1.0 / D, bias=eps[:]).then_inc(ln_ready, 1)
            act.wait_ge(ln_ready, NORMS * HEADS + 2)
            act.activation(rstd2[:], ln_r2[:], ACT.Exp, scale=-0.5).then_inc(r_ready, 1)
            for g in range(4):
                act.wait_ge(xf_ready, 4 + g + 1)
                act.activation(x_hi[:, 4 * g:4 * g + 4, 0:T], x2f[:, 4 * g:4 * g + 4, :], ACT.Copy) \
                    .then_inc(x_hi_ready, 1)

            def route_head(h, first):
                for p in range(2):
                    step(split_hi, act, BASE_D // 4 + h, 2 * p)
                    act.wait_ge(chunk_used, BASE_D + 4 * h + 2 * p + 2)
                    act.activation(q_sb[:, p, :], blk[p][:, 0:T], ACT.Copy).then_inc(q_ready, 1)
                    step(split_hi, act, BASE_D // 4 + h, 2 * p + 1)
                for p in range(2):
                    act.wait_ge(ps_ready, 2 * h + p + 1)
                    if not first:
                        act.wait_ge(routed, 2 * h)
                    act.activation(s_sb[:, p::2, :], sc[p][:, 0:T].rearrange("p (a b) -> p a b", a=TT), ACT.Copy) \
                        .then_inc(ssb_ready, 1)
                act.wait_ge(neg_ready, h + 1)
                for tt in range(TT):
                    act.activation(g_e[:, tt, :], best[:, tt, :], ACT.Exp, bias=neg_best[:, tt:tt + 1],
                                   accum_out=g_sum[:, tt:tt + 1]).then_inc(g_exp_ready, 1)
            route_head(0, True)
            with act.Fori(1, HEADS) as h:
                route_head(h, False)
            q0 = BASE_E // 4
            split_hi(act, q0, 3)

            with act.Fori(0, T // 8) as i:
                for k in range(2):
                    act.wait_ge(table_done, 8 * i + 4 * k + 4)
                    act.activation(w2[:, :, bass.ds(8 * i + 4 * k, 4)],
                                   bank[6 + k][:].rearrange("p (t e) -> p e t", t=4), ACT.Copy).then_inc(table_ready, 1)

            def expert(b, par, used):
                act.wait_ge(chunk_used, used)
                act.activation(gelu[:], up[:, 0:T], ACT.Gelu_apprx_tanh).then_inc(gelu_ready, 1)
                act.wait_ge(pf_ready, b + 1)
                act.activation(p_hi[:, par, :], p_f[:], ACT.Copy).then_inc(p_hi_ready, 1)

            expert(0, 0, BASE_E + 2)

            def round_(b, par):
                split_hi(act, q0 + b, 0)
                split_hi(act, q0 + b, 1)
                expert(b, par, BASE_E + 4 * b)
                split_hi(act, q0 + b, 2)
                split_hi(act, q0 + b, 3)
            with act.Fori(0, P // 2 - 1) as i:
                round_(2 * i + 1, 1)
                round_(2 * i + 2, 0)
            round_(P - 1, 1)

        @block.vector
        def _(dve):
            dve.memset(eps[:], EPS).then_inc(consts_set, 1)
            dve.wait_ge(lam_in, 16)
            for k in range(2):
                dve.tensor_tensor_reduce(lam_w[:], lam_v[:, 2 * k, :], lam_v[:, 2 * k + 1, :], 1.0, 0.0,
                                         ALU.mult, ALU.add, lam_e[:, k:k + 1]).then_inc(lam_dots, 1)
                dve.wait_ge(lam_dots, k + 1)
            dve.wait_ge(lam_exp, 1)
            dve.scalar_tensor_tensor(neg_lam[:], lam_e[:, 1:2], -LAM_INIT, lam_e[:, 0:1], ALU.add, ALU.subtract) \
                .then_inc(lam_done, 1)
            dve.wait_ge(const_in, 7 * 16)
            dve.tensor_scalar(gain[:, GQD:GQD + 1], gain[:, GQD:GQD + 1], DH ** -0.5, None, ALU.mult).then_inc(lam_step, 1)
            dve.tensor_scalar(gain[:, GQN:GQN + 1], gain[:, GQN:GQN + 1], DH ** -0.5, None, ALU.mult).then_inc(lam_step, 1)
            dve.tensor_scalar(gain[:, GOD:GOD + 1], gain[:, GOD:GOD + 1], 1.0 - LAM_INIT, None, ALU.mult).then_inc(lam_step, 1)
            dve.wait_ge(lam_step, 3)
            dve.wait_ge(lam_done, 1)
            dve.wait_ge(r_ready, 1)
            for kc in range(KC):
                ins = dve.scalar_tensor_tensor(xf[:, kc, :], h_t[:, kc, :], gain[:, G1 + kc:G1 + kc + 1], rstd[:],
                                               ALU.mult, ALU.mult)
                if kc % 4 == 3:
                    ins.then_inc(xf_ready, 1)
            for g in range(4):
                if g == 0:
                    for j in range(AHEAD):
                        split_lo_at(dve, j, j)
                dve.wait_ge(x_hi_ready, g + 1)
                dve.tensor_tensor(x_lo[:, 4 * g:4 * g + 4, :], xf[:, 4 * g:4 * g + 4, :],
                                  x_hi[:, 4 * g:4 * g + 4, :].bitcast(F32), ALU.subtract).then_inc(x_lo_ready, 1)

            def head(h, first):
                def scale(i):
                    dve.wait_ge(r_ready, NORMS * h + i + 2)
                    col = (GQD, GKD, GQN, GKN)[i]
                    n = NORM_COLS[i]
                    dve.scalar_tensor_tensor(qk[:, i, 0:n], blk[NORM_BLOCK[i] % 2][:, 0:n], gain[:, col:col + 1],
                                             rstd[:, 0:n], ALU.mult, ALU.mult).then_inc(normed, 1)

                def v_rows(i):
                    dve.wait_ge(v_turned, 2 * h + i + 1)
                    if not first:
                        dve.wait_ge(pv_done, 3 * h - (2 if i == 0 else 0))
                    dve.tensor_copy(v_tok[:, i, :, :].rearrange("p a b -> p (a b)"), turn[:, 0:2 * P]).then_inc(v_ready, 1)
                    dve.tensor_copy(v_meta[:, i, :], turn_m[0:META, 0:P]).then_inc(v_ready, 1)

                def maxima(u0):
                    buf = t_da if u0 < 4 else t_na
                    for u in (u0, u0 + 1):
                        wait_alone(dve, s_ready, 8 * h + u + 1)
                        bias = da_bias[:, u // 2, :] if u < 4 else na_bias[:, u % 4, :]
                        dve.tensor_tensor_reduce(buf[:, u % 4, :], sc[u % 2][:, 0:L], bias, 1.0, MASKED,
                                                 ALU.add, ALU.max, stat_max[:, u:u + 1]).then_inc(max_ready, 1)
                    dve.wait_ge(max_ready, 8 * h + u0 + 2)
                    dve.tensor_scalar(stat_neg[:, u0:u0 + 2], stat_max[:, u0:u0 + 2], -1.0, None, ALU.mult) \
                        .then_inc(t_ready, 1)

                def gate(k):
                    dve.wait_ge(gate_exp, 4 * h + k + 1)
                    dve.tensor_scalar(gate_e[:], gate_e[:], 1.0, None, ALU.add).then_inc(gate_den, 1)
                    dve.wait_ge(gate_den, 4 * h + k + 1)
                    dve.reciprocal(gates[:, (k // 2) * KC + 2 * h + k % 2, :], gate_e[:]).then_inc(gate_ready, 1)

                def mix_da():
                    dve.wait_ge(p_ready, 8 * h + 4)
                    dve.reciprocal(stat_inv[:, 0:4], stat_sum[:, 0:4]).then_inc(inv_ready, 1)
                    dve.wait_ge(inv_ready, 2 * h + 1)
                    for tt in range(TT):
                        dve.tensor_scalar(t_da[:, 2 * tt + 1, :], t_da[:, 2 * tt + 1, :],
                                          stat_inv[:, 2 * tt + 1:2 * tt + 2], neg_lam[:], ALU.mult, ALU.mult) \
                            .then_inc(mix_half, 1)
                    for tt in range(TT):
                        dve.wait_ge(mix_half, 2 * h + tt + 1)
                        ins = dve.scalar_tensor_tensor(t_da[:, 2 * tt, :], t_da[:, 2 * tt, :],
                                                       stat_inv[:, 2 * tt:2 * tt + 1], t_da[:, 2 * tt + 1, :],
                                                       ALU.mult, ALU.add)
                        ins.then_inc(p_normed, 1)

                def norm_na():
                    dve.wait_ge(p_ready, 8 * h + 8)
                    dve.reciprocal(stat_inv[:, 4:8], stat_sum[:, 4:8]).then_inc(inv_ready, 1)
                    dve.wait_ge(inv_ready, 2 * h + 2)
                    for u in (0, 2, 1, 3):
                        dve.tensor_scalar(t_na[:, u, :], t_na[:, u, :], stat_inv[:, 4 + u:5 + u], None, ALU.mult) \
                            .then_inc(p_normed, 1)

                def tick(j):
                    split_lo_at(dve, CHUNKS_A * h + j + AHEAD, (j + AHEAD) % RING_A)

                tick(0); tick(1); tick(2)
                if not first:
                    dve.wait_ge(p_turned, 3 * h)
                    dve.wait_ge(da_bias_ready, h)
                tick(3); scale(0)
                tick(4); tick(5); scale(1)
                tick(6); v_rows(0); maxima(0)
                tick(7); maxima(2)
                tick(8); mix_da(); tick(9); scale(2)
                tick(10); tick(11); scale(3)
                tick(12); v_rows(1)
                dve.wait_ge(na_bias_ready, 1 + 4 * (h + 1))
                maxima(4)
                tick(13)
                dve.wait_ge(r_ready, NORMS * h + 6)
                if not first:
                    dve.wait_ge(o_hi_ready, 2 * h)
                dve.scalar_tensor_tensor(o_f[:], att[:, 0:T], gain[:, GOD:GOD + 1], rstd[:, 0:T],
                                         ALU.mult, ALU.mult).then_inc(normed, 1)
                maxima(6)
                tick(14); gate(0)
                dve.wait_ge(o_hi_ready, 2 * h + 1)
                dve.tensor_tensor(o_lo[:, h, :], o_f[:], o_hi[:, h, :].bitcast(F32), ALU.subtract).then_inc(o_lo_ready, 1)
                tick(15); norm_na()
                tick(16); gate(1); tick(17)
                tick(18); gate(2); tick(19)
                dve.wait_ge(o_hi_ready, 2 * h + 2)
                dve.tensor_tensor(o_lo[:, HEADS + h, :], att[:, 0:T], o_hi[:, HEADS + h, :].bitcast(F32),
                                  ALU.subtract).then_inc(o_lo_ready, 1)
                gate(3)

            head(0, True)
            with dve.Fori(1, HEADS) as h:
                head(h, False)

            with dve.Fori(0, HEADS) as i:
                for j in range(4):
                    if j % 2 == 1:
                        k = j // 2
                        dve.wait_ge(chunk_used, BASE_B + 4 * i + 2 * k + 2)
                        yd, yn = (blk, sc)[k]
                        dve.tensor_tensor(m_a[:, k, :], yd[:, 0:T], gates[:, 2 * i + k, :], ALU.mult).then_inc(m_parts, 1)
                        dve.tensor_tensor(m_b[:, k, :], yn[:, 0:T], gates[:, KC + 2 * i + k, :], ALU.mult).then_inc(m_parts, 1)
                        dve.wait_ge(m_parts, 4 * i + 2 * k + 2)
                        dve.tensor_tensor(m_f[:, k, :], m_a[:, k, :], m_b[:, k, :], ALU.add).then_inc(m_ready, 1)
                        dve.wait_ge(m_hi_ready, 2 * i + k + 1)
                        dve.tensor_tensor(m_lo[:, 2 * i + k, :], m_f[:, k, :], m_hi[:, 2 * i + k, :].bitcast(F32),
                                          ALU.subtract).then_inc(m_lo_ready, 1)
                    step(split_lo, dve, BASE_B // 4 + i, j)

            with dve.Fori(0, HEADS) as i:
                for j in range(4):
                    if j % 2 == 1:
                        k = j // 2
                        dve.wait_ge(chunk_used, BASE_C + 4 * i + 2 * k + 2)
                        dve.tensor_tensor(h_t[:, 2 * i + k, 0:T], blk[k][:, 0:T], h_t[:, 2 * i + k, 0:T], ALU.add) \
                            .then_inc(h2_ready, 1)
                    step(split_lo, dve, BASE_C // 4 + i, j)

            dve.wait_ge(r_ready, NORMS * HEADS + 2)
            dve.wait_ge(h2_ready, KC)
            for kc in range(KC):
                ins = dve.scalar_tensor_tensor(x2f[:, kc, :], h_t[:, kc, 0:T], gain[:, G2 + kc:G2 + kc + 1], rstd2[:],
                                               ALU.mult, ALU.mult)
                if kc % 4 == 3:
                    ins.then_inc(xf_ready, 1)
            for g in range(4):
                dve.wait_ge(x_hi_ready, 4 + g + 1)
                dve.tensor_tensor(x_lo[:, 4 * g:4 * g + 4, 0:T], x2f[:, 4 * g:4 * g + 4, :],
                                  x_hi[:, 4 * g:4 * g + 4, 0:T].bitcast(F32), ALU.subtract).then_inc(x_lo_ready, 1)

            with dve.Fori(0, HEADS) as h:
                for j in range(4):
                    step(split_lo, dve, BASE_D // 4 + h, j)
                wait_alone(dve, ssb_ready, 2 * h + 2)
                lists = range(4)
                for n in lists:
                    dve.max(top[:, n, 0:8], s_sb[:, n, :]).then_inc(top_step, 1)
                for n in lists:
                    wait_alone(dve, top_step, 20 * h + n + 1)
                    dve.match_replace(s_rest[:, n, :], top[:, n, 0:8], s_sb[:, n, :], LOWEST).then_inc(top_step, 1)
                for n in lists:
                    wait_alone(dve, top_step, 20 * h + 4 + n + 1)
                    dve.max(top[:, n, 8:16], s_rest[:, n, :]).then_inc(top_step, 1)
                for n in lists:
                    dve.max_index(top_i[:, n, 0:8], top[:, n, 0:8], s_sb[:, n, :]).then_inc(top_step, 1)
                for n in lists:
                    wait_alone(dve, top_step, 20 * h + 8 + n + 1)
                    dve.max_index(top_i[:, n, 8:16], top[:, n, 8:16], s_rest[:, n, :]).then_inc(top_step, 1)
                dve.tensor_tensor(cand[:].rearrange("p t (a b) -> p t a b", a=TOPK),
                                  top[:, 0::2, :].unsqueeze(3).broadcast_to([P, TT, TOPK, TOPK]),
                                  top[:, 1::2, :].unsqueeze(2).broadcast_to([P, TT, TOPK, TOPK]),
                                  ALU.add).then_inc(best_step, 1)
                dve.wait_ge(top_step, 20 * h + 20)
                dve.tensor_copy(top_f[:], top_i[:]).then_inc(decode_step, 1)
                wait_alone(dve, best_step, 11 * h + 1)
                for tt in range(TT):
                    dve.max(best[:, tt, 0:8], cand[:, tt, :]).then_inc(best_step, 1)
                for tt in range(TT):
                    wait_alone(dve, best_step, 11 * h + 2 + tt)
                    dve.match_replace(cand_rest[:, tt, :], best[:, tt, 0:8], cand[:, tt, :], LOWEST).then_inc(best_step, 1)
                for tt in range(TT):
                    wait_alone(dve, best_step, 11 * h + 4 + tt)
                    dve.max(best[:, tt, 8:16], cand_rest[:, tt, :]).then_inc(best_step, 1)
                dve.wait_ge(best_step, 11 * h + 7)
                dve.tensor_scalar(neg_best[:], best[:, :, 0], -1.0, None, ALU.mult).then_inc(neg_ready, 1)
                for tt in range(TT):
                    dve.max_index(best_i[:, tt, 0:8], best[:, tt, 0:8], cand[:, tt, :]).then_inc(best_step, 1)
                for tt in range(TT):
                    dve.max_index(best_i[:, tt, 8:16], best[:, tt, 8:16], cand_rest[:, tt, :]).then_inc(best_step, 1)
                dve.wait_ge(best_step, 11 * h + 11)
                dve.tensor_scalar(pos_i[:, :, 0, :], best_i[:], 4, None, ALU.logical_shift_right).then_inc(decode_step, 1)
                dve.tensor_scalar(pos_i[:, :, 1, :], best_i[:], 15, None, ALU.bitwise_and).then_inc(decode_step, 1)
                dve.wait_ge(decode_step, 6 * h + 3)
                dve.tensor_copy(pos_f[:], pos_i[:]).then_inc(decode_step, 1)
                dve.wait_ge(decode_step, 6 * h + 4)
                dve.tensor_tensor(eq[:], pos_f[:].rearrange("p t l k -> p (t l) k").unsqueeze(3)
                                  .broadcast_to([P, 4, TOPK, TOPK]),
                                  iota[:, 0:TOPK].unsqueeze(1).unsqueeze(1).broadcast_to([P, 4, TOPK, TOPK]),
                                  ALU.is_equal).then_inc(decode_step, 1)
                dve.wait_ge(decode_step, 6 * h + 5)
                dve.tensor_tensor(eqv[:], eq[:], top_f[:].unsqueeze(2).broadcast_to([P, 4, TOPK, TOPK]),
                                  ALU.mult).then_inc(decode_step, 1)
                dve.wait_ge(g_exp_ready, 2 * h + 2)
                dve.reciprocal(g_inv[:], g_sum[:]).then_inc(g_inv_ready, 1)
                dve.wait_ge(decode_step, 6 * h + 6)
                for l in range(2):
                    dve.tensor_reduce(route[:, l, :, bass.ds(h * TOPK, TOPK)], eqv[:, l::2, :, :], AX.X, ALU.add) \
                        .then_inc(routed, 1)
                dve.wait_ge(g_inv_ready, h + 1)
                for tt in range(TT):
                    dve.tensor_scalar(route[:, 2, tt, bass.ds(h * TOPK, TOPK)], g_e[:, tt, :], g_inv[:, tt:tt + 1], None,
                                      ALU.mult).then_inc(route_ready, 1)

            for r in range(3):
                dve.wait_ge(route_turned, r + 1)
                dve.tensor_copy(route_t[:, r, :], (turn, turn_m, att)[r][:, 0:T]).then_inc(route_ready, 1)
            for k in range(2):
                dve.wait_ge(seeded, 7 + k)
                dve.tensor_copy(acc[:, k, :], bank[6 + k][:]).then_inc(acc_ready, 1)
            q0 = BASE_E // 4
            split_lo(dve, q0, 3)
            dve.wait_ge(route_ready, 2 * HEADS + 3)

            def hot(i, k, first):
                t = 4 * i + k
                if not first:
                    dve.wait_ge(table_done, 4 * i + k - 3)
                dve.tensor_scalar(hot1[:, k, :], iota[:], route_t[:, 0, bass.ds(t, 1)], route_t[:, 2, bass.ds(t, 1)],
                                  ALU.is_equal, ALU.mult).then_inc(hot_ready, 1)
                dve.tensor_scalar(hot2[:, k, :], iota[:], route_t[:, 1, bass.ds(t, 1)], None,
                                  ALU.is_equal).then_inc(hot_ready, 1)
            for k in range(4):
                hot(0, k, True)
            with dve.Fori(1, T // 4) as i:
                for k in range(4):
                    hot(i, k, False)

            def expert(b, par, first=False):
                if not first:
                    dve.wait_ge(p_lo_ready, b)
                dve.wait_ge(gelu_ready, b + 1)
                dve.tensor_tensor(p_f[:], gelu[:], w2[:, b, :], ALU.mult).then_inc(pf_ready, 1)
                dve.wait_ge(p_hi_ready, b + 1)
                dve.tensor_tensor(p_lo[:, par, :], p_f[:], p_hi[:, par, :].bitcast(F32), ALU.subtract).then_inc(p_lo_ready, 1)

            def add_spare(b, k, used=None):
                if k == 0:
                    dve.wait_ge(spare_done, b + 1)
                else:
                    dve.wait_ge(chunk_used, used)
                dve.tensor_tensor(acc[:, k, :], spare[:], acc[:, k, :], ALU.add).then_inc(spare_added, 1)

            dve.wait_ge(table_ready, T // 4)
            dve.wait_ge(acc_ready, 2)
            expert(0, 0, True)

            def round_(b, par):
                split_lo(dve, q0 + b, 0)
                split_lo(dve, q0 + b, 1)
                expert(b, par)
                split_lo(dve, q0 + b, 2)
                add_spare(b - 1, 0)
                split_lo(dve, q0 + b, 3)
                add_spare(b - 1, 1, BASE_E + 4 * b + 2)
            with dve.Fori(0, P // 2 - 1) as i:
                round_(2 * i + 1, 1)
                round_(2 * i + 2, 0)
            round_(P - 1, 1)
            add_spare(P - 1, 0)
            add_spare(P - 1, 1, N_CHUNKS)
            dve.wait_ge(chunk_used, N_CHUNKS)
            for k in range(6):
                dve.tensor_copy(out_sb[:, k, :], held[k][:]).then_inc(out_ready, 1)

        @block.tensor
        def _(pe):
            pe.wait_ge(const_in, 7 * 16)
            for kc in range(KC):
                if kc % 4 == 0:
                    pe.wait_ge(sq_ready, kc // 4 + 1)
                ins = pe.matmul(ms[:, 0:L], ones[:], sq_big[:, kc, :], start=kc == 0, stop=kc == KC - 1)
            ins.then_inc(ms_ready, 1)
            pe.wait_ge(x_lo_ready, 4)

            def head(h, first):
                def chunk(c):
                    j, half = c // 2, c % 2
                    w = T if j in (0, 3) or j > 5 else L
                    if half == 0:
                        free_bank(j)
                    products(pe, CHUNKS_A * h + c, c % RING_A, blk[j % 2][:, 0:w], x_hi, x_lo, 8 * half, w,
                             half == 0, half == 1)

                def free_bank(j):
                    if j < 2:
                        if not first:
                            pe.wait_ge(gate_exp, 4 * h - 1 + j)
                    elif j in (2, 3, 5, 6):
                        pe.wait_ge(normed, NORMS * h + {2: 1, 3: 2, 5: 3, 6: 4}[j])
                    elif j in (4, 7):
                        pe.wait_ge(vt_ready, 2 * h + (1 if j == 4 else 2))
                    else:
                        pe.wait_ge(gate_exp, 4 * h + j - 7)

                def mean_square(i):
                    w = NORM_COLS[i]
                    pe.wait_ge(sq_ready, NORMS * h + 4 + i + 1)
                    pe.matmul(ms[:, 0:w], (ones if i == 4 else pair_ones)[:], sq[:, 0:w], start=True, stop=True) \
                        .then_inc(ms_ready, 1)

                def turn_v(i):
                    pe.wait_ge(vt_ready, 2 * h + i + 1)
                    if i == 1:
                        pe.wait_ge(pt_ready, 6 * h + 2)
                    elif not first:
                        pe.wait_ge(pt_ready, 6 * h)
                    pe.transpose(turn[:, 0:P], v_t[:, 0:P], ident[:])
                    pe.transpose(turn[:, P:2 * P], v_t[:, P:2 * P], ident[:])
                    pe.transpose(turn_m[0:META, 0:P], v_t[:, T:L], ident[:]).then_inc(v_turned, 1)

                def score(u):
                    if u == 0:
                        pe.wait_ge(normed, NORMS * h + 2)
                    if u == 4:
                        pe.wait_ge(normed, NORMS * h + 4)
                    if not (first and u < 2):
                        pe.wait_ge(max_ready, 8 * h + u - 1)
                    q, k = (0, 1) if u < 4 else (2, 3)
                    half, tt = u % 2, (u % 4) // 2
                    rows = slice(half * DH, (half + 1) * DH)
                    pe.matmul(sc[u % 2][:, 0:L], qk[rows, q, tt * P:(tt + 1) * P], qk[rows, k, :],
                              start=True, stop=True).then_inc(s_ready, 1)

                def turn_p(i):
                    if i == 0:
                        pe.wait_ge(v_ready, 4 * h + 2)
                        pe.wait_ge(p_normed, 6 * h + 2)
                    elif i == 1:
                        pe.wait_ge(v_ready, 4 * h + 4)
                        pe.wait_ge(p_normed, 6 * h + 4)
                    else:
                        pe.wait_ge(pt_ready, 6 * h + 4)
                        pe.wait_ge(p_normed, 6 * h + 6)
                    for tt in range(TT):
                        src = t_da[:, 2 * tt, :] if i == 0 else t_na[:, 2 * tt + i - 1, :]
                        for kt in range(2):
                            pe.transpose(turn[:, kt * T + tt * P:kt * T + (tt + 1) * P], src[:, kt * P:(kt + 1) * P], ident[:])
                        ins = pe.transpose(turn_m[0:META, tt * P:(tt + 1) * P], src[:, T:L], ident[:])
                    ins.then_inc(p_turned, 1)

                def pv(i):
                    pe.wait_ge(pt_ready, 6 * h + 2 * i + 2)
                    if i == 0:
                        if not first:
                            pe.wait_ge(o_lo_ready, 2 * h)
                    elif i == 1:
                        pe.wait_ge(normed, NORMS * h + 5)
                    rows = slice(0, P) if i == 0 else slice((i - 1) * DH, i * DH)
                    n = 0 if i == 0 else 1
                    for kt in range(2):
                        pe.matmul(att[rows, 0:T], v_tok[:, n, kt, rows], p_t[:, i, kt, :], start=kt == 0, stop=False)
                    pe.matmul(att[rows, 0:T], v_meta[:, n, rows], p_meta[:, i, :], start=False, stop=True) \
                        .then_inc(pv_done, 1)

                chunk(0); chunk(1); chunk(2); mean_square(0)
                chunk(3); chunk(4); mean_square(1)
                chunk(5); chunk(6); turn_v(0); score(0); score(1)
                chunk(7); score(2); score(3)
                chunk(8); mean_square(2)
                chunk(9); turn_p(0)
                chunk(10); mean_square(3); pv(0)
                chunk(11); chunk(12); turn_v(1); mean_square(4); score(4); score(5)
                chunk(13); score(6); score(7)
                chunk(14); chunk(15); chunk(16); turn_p(1)
                chunk(17); turn_p(2); pv(1)
                chunk(18); pv(2)
                chunk(19)

            head(0, True)
            with pe.Fori(1, HEADS) as h:
                head(h, False)

            pe.wait_ge(o_lo_ready, 2 * HEADS)
            pe.wait_ge(gate_exp, 4 * HEADS)
            pe.wait_ge(max_ready, 8 * HEADS)

            def branch_rows(i, first):
                for k in range(2):
                    if not first:
                        pe.wait_ge(m_parts, 4 * i - 2 + 2 * k)
                    for j in range(2):
                        products(pe, BASE_B + 4 * i + 2 * k + j, 2 * k + j, (blk, sc)[k][j][:, 0:T], o_hi, o_lo, j * HEADS, T,
                                 True, True)
            branch_rows(0, True)
            with pe.Fori(1, HEADS) as i:
                branch_rows(i, False)

            def out_rows(i, first, last):
                for k in range(2):
                    if not first:
                        pe.wait_ge(h2_ready, 2 * i + k - 1)
                    for s in range(2):
                        products(pe, BASE_C + 4 * i + 2 * k + s, 2 * k + s, blk[k][:, 0:T], m_hi, m_lo, 8 * s, T, s == 0, s == 1)
                    if k == 0 and first:
                        continue
                    square_sum(2 * i + k - 1, (k + 1) % 2, first, False)
                if last:
                    square_sum(2 * i + 1, 1, False, True)

            def square_sum(n, par, start, stop):
                pe.wait_ge(sq2_ready, n + 1)
                pe.matmul(ms[:, 0:T], ones[:], sq2[:, par, :], start=start, stop=stop).then_inc(sq2_used, 1)

            pe.wait_ge(m_lo_ready, KC)
            out_rows(0, True, False)
            with pe.Fori(1, HEADS - 1) as i:
                out_rows(i, False, False)
            out_rows(HEADS - 1, False, True)

            pe.wait_ge(subk_in, 16)
            pe.wait_ge(x_lo_ready, 8)
            pe.wait_ge(h2_ready, KC)

            def query_head(h, first):
                for p in range(2):
                    if not first and p == 0:
                        pe.wait_ge(q_ready, 2 * h)
                    for s in range(2):
                        products(pe, BASE_D + 4 * h + 2 * p + s, 2 * p + s, blk[p][:, 0:T], x_hi, x_lo, 8 * s, T, s == 0, s == 1)
                if not first:
                    pe.wait_ge(ssb_ready, 2 * h)
                for p in range(2):
                    pe.wait_ge(q_ready, 2 * h + p + 1)
                    for tt in range(TT):
                        ins = pe.matmul(sc[p][:, tt * P:(tt + 1) * P], q_sb[:, p, tt * P:(tt + 1) * P], subk[:, p, :],
                                        start=True, stop=True)
                    ins.then_inc(ps_ready, 1)
            query_head(0, True)
            with pe.Fori(1, HEADS) as h:
                query_head(h, False)

            pe.wait_ge(routed, 2 * HEADS)
            pe.wait_ge(route_ready, 2 * HEADS)
            for r in range(3):
                for tt in range(TT):
                    ins = pe.transpose((turn, turn_m, att)[r][:, tt * P:(tt + 1) * P], route[:, r, tt, :], ident[:])
                ins.then_inc(route_turned, 1)
            pe.wait_ge(ssb_ready, 2 * HEADS)
            pe.wait_ge(route_ready, 2 * HEADS + 3)

            for k in range(8):
                tt, dc = k // 4, k % 4
                for n in range(4):
                    ins = pe.matmul(bank[k][:, n * P:(n + 1) * P], h_t[:, 4 * dc + n, tt * P:(tt + 1) * P], ident[:],
                                    start=n == 0, stop=True, skip_group_check=True)
                ins.then_inc(seeded, 1)
            pe.wait_ge(acc_ready, 2)

            def table(t4, k, first):
                if not first:
                    pe.wait_ge(table_ready, t4 - 1)
                for n in range(4):
                    pe.wait_ge(hot_ready, 8 * t4 + 2 * n + 2)
                    pe.matmul(bank[6 + k][:, n * P:(n + 1) * P], hot2[:, n, :], hot1[:, n, :], start=True, stop=True) \
                        .then_inc(table_done, 1)
            table(0, 0, True)
            table(1, 1, True)
            with pe.Fori(1, T // 8) as i:
                table(2 * i, 0, False)
                table(2 * i + 1, 1, False)

            q0 = BASE_E // 4

            def up_rows(b, quad, slot, first):
                if first:
                    pe.wait_ge(table_ready, T // 4)
                else:
                    pe.wait_ge(gelu_ready, b)
                for s in range(2):
                    products(pe, 4 * quad + slot + s, slot + s, up[:, 0:T], x_hi, x_lo, 8 * s, T, s == 0, s == 1)

            def down_tile(outp, tt, par, slot, dcl, start, stop):
                a_hi = p_hi[:, par, tt * P:(tt + 1) * P]
                a_lo = p_lo[:, par, tt * P:(tt + 1) * P]
                cols = slice(dcl * 512, (dcl + 1) * 512)
                pe.matmul(outp, a_hi, chunk_lo[slot][:, cols], start=start, stop=False, skip_group_check=True)
                pe.matmul(outp, a_lo, chunk_hi[slot][:, cols], start=False, stop=False, skip_group_check=True)
                return pe.matmul(outp, a_hi, chunk_hi[slot][:, cols], start=False, stop=stop, skip_group_check=True)

            def down_rows(b, par, quad, slot, first):
                pe.wait_ge(p_lo_ready, b + 1)
                pe.wait_ge(lo_ready, 4 * quad + slot + 1)
                for k in (0, 1, 4, 5):
                    ins = down_tile(held[k][:], k // 4, par, slot, k % 4, False, True)
                ins.then_inc(chunk_used, 1)
                slot += 1
                pe.wait_ge(lo_ready, 4 * quad + slot + 1)
                for n, k in enumerate((6, 2, 3, 7)):
                    if k >= 6:
                        if not (first and k == 6):
                            pe.wait_ge(spare_added, 2 * b + k - 6)
                        ins = down_tile(spare[:], 1, par, slot, k - 6, True, True)
                        if k == 6:
                            ins.then_inc(spare_done, 1)
                    else:
                        ins = down_tile(held[k][:], 0, par, slot, k - 2, False, True)
                ins.then_inc(chunk_used, 1)

            up_rows(0, q0, 0, True)

            def round_(b, par_prev, first=False):
                up_rows(b, q0 - 1 + b, 2, False)
                down_rows(b - 1, par_prev, q0 + b, 0, first)
            round_(1, 0, True)
            round_(2, 1)
            with pe.Fori(1, P // 2 - 1) as i:
                round_(2 * i + 1, 0)
                round_(2 * i + 2, 1)
            round_(P - 1, 0)
            down_rows(P - 1, 1, q0 + P - 1, 2, False)


def kernel(**inputs):
    import concourse.bacc as bacc
    from concourse.bass_utils import run_bass_kernel_spmd

    f = {k: np.asarray(v) for k, v in inputs.items()}

    def by_block(w, kc):
        n = w.shape[1] // P
        return w.reshape(kc, P, n, P).transpose(2, 1, 0, 3)

    def chunks(w):
        n, _, kc, _ = w.shape
        return w.reshape(n, P, kc // 8, 8, P).transpose(0, 2, 1, 3, 4).reshape(n * kc // 8, P, CH)

    arrays = {}
    h = np.concatenate([f["x"][0], f["meta_tokens"]], axis=0)
    arrays["h_turned"] = h.reshape(L, KC, P).transpose(2, 1, 0)
    def twice(g):
        return np.concatenate([g[0], g[0]])[:, None]
    arrays["gains"] = np.concatenate(
        [f["norm1_g"][0].reshape(KC, P).T, f["norm2_g"][0].reshape(KC, P).T, twice(f["da_q_norm_g"]),
         twice(f["da_k_norm_g"]), twice(f["na_q_norm_g"]), twice(f["na_k_norm_g"]), f["da_out_norm_g"][0][:, None]], axis=1)
    arrays["lambdas"] = np.broadcast_to(
        np.stack([f["lambda_q1"][0], f["lambda_k1"][0], f["lambda_q2"][0], f["lambda_k2"][0]])[None], (P, 4, DH))
    q = (META + np.arange(T)).reshape(TT, P).T
    k = np.concatenate([META + np.arange(T), np.arange(META)])
    arrays["alibi"] = (-0.5 * np.abs(q[:, :, None] - k[None, None, :])).astype(np.float32)
    c = np.arange(P) % GRID_W
    first = np.clip(c - WIN_W // 2, 0, GRID_W - WIN_W)[:, None]
    kc_ = (np.arange(T) % GRID_W)[None]
    arrays["na_mask"] = np.where((kc_ >= first) & (kc_ < first + WIN_W), 0.0, MASKED).astype(np.float32)
    pad = np.zeros((2 * HEADS, RPB_H, RPB_PITCH), np.float32)
    pad[:, :, GRID_W - WIN_W:GRID_W - WIN_W + RPB_W] = f["na_rpb"][0]
    arrays["rpb"] = np.broadcast_to(pad.reshape(HEADS, 2, RPB_H, 1, RPB_PITCH), (HEADS, 2, RPB_H, GRID_W, RPB_PITCH))
    arrays["ident_d"] = np.eye(P, dtype=np.float32)
    arrays["ones_d"] = np.ones((P, P), np.float32)
    arrays["pair_ones_d"] = np.kron(np.eye(2), np.ones((DH, DH))).astype(np.float32)
    arrays["iota_d"] = np.ascontiguousarray(np.broadcast_to(np.arange(P, dtype=np.float32), (P, P)))
    arrays["sub_keys"] = f["peer_sub_keys"][0].transpose(2, 0, 1)
    w = by_block(f["w_in"][0], KC)
    order = [b for n in range(HEADS) for b in
             (n, 8 + n, 16 + n, 24 + n, 32 + n, 40 + n, 48 + 2 * n, 49 + 2 * n, 64 + 2 * n, 65 + 2 * n)]
    arrays["w_in"] = chunks(w[order])
    arrays["w_branch"] = np.stack([chunks(by_block(f["w_branch_da"][0], 8)), chunks(by_block(f["w_branch_na"][0], 8))],
                                  axis=1).reshape(2 * KC, P, CH)
    arrays["w_out"] = chunks(by_block(f["w_out"][0], KC))
    arrays["w_query"] = chunks(by_block(f["peer_w_query"][0], KC))
    arrays["peer_u"] = chunks(f["peer_u"][0].reshape(P, P, KC, P).transpose(0, 3, 2, 1))
    arrays["peer_v"] = f["peer_v"][0].reshape(P, P, 2, CH).transpose(0, 2, 1, 3)

    nc = bacc.Bacc("TRN2", target_bir_lowering=False, num_devices=1)
    feeds, args = {}, []
    for name in ("h_turned", "gains", "lambdas", "alibi", "na_mask", "rpb", "ident_d", "ones_d", "pair_ones_d",
                 "iota_d", "sub_keys", "w_in", "w_branch", "w_out", "w_query", "peer_u", "peer_v"):
        a = np.ascontiguousarray(arrays[name])
        feeds[f"in_{name}"] = a
        args.append(nc.dram_tensor(f"in_{name}", a.shape, mybir.dt.from_np(a.dtype), kind="ExternalInput").ap())
    out = nc.dram_tensor("out_h", (T, D), F32, kind="ExternalOutput").ap()
    block_kernel(nc, *args, out)
    r = run_bass_kernel_spmd(nc, [feeds], core_ids=[0])
    return r.results[0]["out_h"][None]
```

```python
from contextlib import ExitStack

import numpy as np

import concourse.bass as bass
from concourse import mybir

F32 = mybir.dt.float32
F32R = mybir.dt.float32r
U32 = mybir.dt.uint32
ALU = mybir.AluOpType
ACT = mybir.ActivationFunctionType
AX = mybir.AxisListType

P = 128
D = 2048
KC = D // P
T = 256
META = 16
L = T + META
TT = T // P
HEADS = 8
DH = 64
GRID_W = 64
ROWS = T // GRID_W
RPB_H, RPB_W = 15, 31
RPB_PITCH = 128
WIN_W = 16
TOPK = 16
EPS = 1e-6
LAM_INIT = 0.2
MASKED = -1e30
LOWEST = -3.0e38

CH = 1024
RING = 4
RING_A = 5
BLOCKS_A = 10
CHUNKS_A = 2 * BLOCKS_A
BASE_B = HEADS * CHUNKS_A
BASE_C = BASE_B + 2 * KC
BASE_D = BASE_C + 2 * KC
EARLY = HEADS + 2
BASE_V = BASE_D + 2 * KC + 2 * EARLY
N_CHUNKS = BASE_D + 2 * KC + 4 * P
AHEAD = 3

G1, G2, GQD, GKD, GQN, GKN, GOD = 0, 16, 32, 33, 34, 35, 36
N_GAINS = 37


def block_kernel(nc, h_turned, gains, lambdas, alibi, na_mask, rpb, ident_d, ones_d, pair_ones_d, iota_d,
                 sub_keys, w_in, w_branch, w_out, w_query, peer_u, peer_v, out):
    ctx = ExitStack()
    with ctx:
        def sem(name):
            return ctx.enter_context(nc.semaphore(name))

        cursor = [16512]

        def place(name, shape, dt, at=None):
            size = int(np.prod(shape[1:])) * 4
            if at is None:
                at = cursor[0]
                cursor[0] += -(-size // 32) * 32
            return nc.alloc_sbuf_tensor_at(name, shape, dt, offset=at)

        x_parts = place("x_parts", [P, KC, 2, L], F32R)
        x_hi, x_lo = x_parts[:, :, 0, :], x_parts[:, :, 1, :]
        chunk_hi, chunk_raw, chunk_lo, at_slot = [], [], [], []
        for s in range(RING_A):
            at_slot.append(cursor[0])
            chunk_hi.append(place(f"chunk_hi{s}", [P, CH], F32R))
            chunk_raw.append(place(f"chunk_raw{s}", [P, CH], F32))
            chunk_lo.append(place(f"chunk_lo{s}", [P, CH], F32R, at=at_slot[s] + CH * 4))
        at_p = at_slot[RING]
        cursor[0] = at_p + 10240
        iota = place("iota", [P, P], F32)
        ident = place("ident", [P, P], F32)
        ones = place("ones", [P, P], F32)
        pair_ones = place("pair_ones", [P, P], F32)
        gain = place("gain", [P, N_GAINS], F32)
        eps = place("eps", [P, 1], F32)
        one = place("one", [P, 1], F32)
        neg_lam = place("neg_lam", [P, 1], F32)
        lam_e = place("lam_e", [P, 2], F32)
        stat_max = place("stat_max", [P, 8], F32)
        stat_neg = place("stat_neg", [P, 8], F32)
        stat_sum = place("stat_sum", [P, 8], F32)
        stat_inv = place("stat_inv", [P, 8], F32)
        at_w = cursor[0]
        assert at_w + P * T * 4 <= nc.sbuf_usable_end, (at_w + P * T * 4, nc.sbuf_usable_end)

        w2 = nc.alloc_sbuf_tensor_at("w2", [P, P, T], F32, offset=at_w)
        cursor[0] = at_w
        gates = place("gates", [P, 2 * KC, T], F32)
        h_t = place("h_t", [P, KC, L], F32)
        o_hi = place("o_hi", [P, 2 * HEADS, T], F32R)
        o_lo = place("o_lo", [P, 2 * HEADS, T], F32R)
        at_scratch = cursor[0]
        da_bias = place("da_bias", [P, TT, L], F32)
        na_bias = place("na_bias", [P, 4, L], F32)
        rpb_t = place("rpb_t", [P, 2, 4, T], F32)
        mask = place("mask", [P, T], F32)
        t_da = place("t_da", [P, 4, L], F32)
        t_na = place("t_na", [P, 4, L], F32)
        sq = place("sq", [P, L], F32)
        ln_r = place("ln_r", [P, L], F32)
        rstd = place("rstd", [P, L], F32)
        qk = place("qk", [P, 4, L], F32)
        v_t = place("v_t", [P, L], F32)
        v_tok = place("v_tok", [P, 2, 2, P], F32)
        v_meta = place("v_meta", [META, 2, P], F32)
        p_t = place("p_t", [P, 3, TT, T], F32)
        p_meta = place("p_meta", [META, 3, T], F32)
        o_f = place("o_f", [P, T], F32)
        gate_e = place("gate_e", [P, T], F32)
        assert cursor[0] <= at_w + P * T * 4
        lam_v = nc.alloc_sbuf_tensor_at("lam_v", [P, 4, DH], F32, offset=at_scratch + 2176)
        lam_w = nc.alloc_sbuf_tensor_at("lam_w", [P, DH], F32, offset=at_scratch + 2176 + 1024)
        sq_big = nc.alloc_sbuf_tensor_at("sq_big", [P, KC, L], F32, offset=at_w)
        xf = nc.alloc_sbuf_tensor_at("xf", [P, KC, L], F32, offset=at_w + 50176)
        cursor[0] = at_scratch
        m_hi = place("m_hi", [P, KC, T], F32R)
        m_lo = place("m_lo", [P, KC, T], F32R)
        m_a = place("m_a", [P, 2, T], F32)
        m_b = place("m_b", [P, 2, T], F32)
        m_f = place("m_f", [P, 2, T], F32)
        sq2 = place("sq2", [P, 2, T], F32)
        x2f = nc.alloc_sbuf_tensor_at("x2f", [P, KC, T], F32, offset=at_w)
        ln_r2 = place("ln_r2", [P, T], F32)
        rstd2 = place("rstd2", [P, T], F32)
        assert EARLY * T * 4 <= 32768
        cursor[0] = at_w + 17408 + 32768
        subk = place("subk", [P, 2, P], F32)
        q_sb = place("q_sb", [P, 2, T], F32)
        s_sb = place("s_sb", [P, 2, 4, P], F32)
        s_rest = place("s_rest", [P, 4, P], F32)
        top = place("top", [P, 4, TOPK], F32)
        top_i = place("top_i", [P, 4, TOPK], U32)
        top_f = place("top_f", [P, 4, TOPK], F32)
        cand = place("cand", [P, TT, TOPK * TOPK], F32)
        cand_rest = place("cand_rest", [P, TT, TOPK * TOPK], F32)
        best = place("best", [P, TT, TOPK], F32)
        best_i = place("best_i", [P, TT, TOPK], U32)
        pos_i = place("pos_i", [P, TT, 2, TOPK], U32)
        pos_f = place("pos_f", [P, TT, 2, TOPK], F32)
        eq = place("eq", [P, 4, TOPK, TOPK], F32)
        eqv = place("eqv", [P, 4, TOPK, TOPK], F32)
        g_sum = place("g_sum", [P, TT, HEADS], F32)
        g_inv = place("g_inv", [P, TT, HEADS], F32)
        route = place("route", [P, 3, TT, P], F32)
        assert cursor[0] <= at_w + P * T * 4
        route_t = nc.alloc_sbuf_tensor_at("route_t", [P, 3, T], F32, offset=at_p)
        hot1 = nc.alloc_sbuf_tensor_at("hot1", [P, 2, 4, P], F32, offset=at_slot[3])
        hot2 = nc.alloc_sbuf_tensor_at("hot2", [P, 2, 4, P], F32, offset=at_slot[3] + 4096)
        hot_sq = nc.alloc_sbuf_tensor_at("hot_sq", [P, 2, P], F32, offset=at_p + 5120)
        p_hi = nc.alloc_sbuf_tensor_at("p_hi", [P, 2, T], F32R, offset=at_p)
        p_lo = nc.alloc_sbuf_tensor_at("p_lo", [P, 2, T], F32R, offset=at_p + 2048)
        gelu = nc.alloc_sbuf_tensor_at("gelu", [P, T], F32, offset=at_p + 4096)
        p_f = nc.alloc_sbuf_tensor_at("p_f", [P, T], F32, offset=at_p + 5120)
        acc = nc.alloc_sbuf_tensor_at("acc", [P, 2, 512], F32, offset=at_p + 6144)
        out_sb = nc.alloc_sbuf_tensor_at("out_sb", [P, 6, 512], F32, offset=at_w)

        bank = [ctx.enter_context(nc.psum_tensor(f"bank{i}", [P, 512], F32)) for i in range(8)]
        blk = [bank[0], bank[1]]
        ms = bank[2]
        sc = [bank[3], bank[4]]
        turn, turn_m, att = bank[5], bank[6], bank[7]
        held = bank[0:6]
        up, spare = bank[6], bank[7]
        turned = [bank[7][:, 0:T], bank[6][:, 0:T], bank[7][:, 0:T]]

        landed = [sem(f"landed{s}") for s in range(RING_A)]
        hi_ready = sem("hi_ready")
        lo_ready = sem("lo_ready")
        chunk_used = sem("chunk_used")
        h_in = [sem(f"h_in{g}") for g in range(4)]
        ones_in, gain_in = sem("ones_in"), sem("gain_in")
        const_in, lam_in, rpb_in = sem("const_in"), sem("lam_in"), [sem("rpb_in0"), sem("rpb_in1")]
        subk_in = sem("subk_in")
        consts_set = sem("consts_set")
        lam_dots, lam_exp, lam_done, lam_step = sem("lam_dots"), sem("lam_exp"), sem("lam_done"), sem("lam_step")
        sq_ready, ms_ready, ln_ready = sem("sq_ready"), sem("ms_ready"), sem("ln_ready")
        r_ready, normed = sem("r_ready"), sem("normed")
        xf_ready, x_hi_ready, x_lo_ready = sem("xf_ready"), sem("x_hi_ready"), sem("x_lo_ready")
        x_lo_pool = sem("x_lo_pool")
        vt_ready, v_turned, v_ready = sem("vt_ready"), sem("v_turned"), sem("v_ready")
        s_ready, max_ready, t_ready = sem("s_ready"), sem("max_ready"), sem("t_ready")
        p_ready, inv_ready, mix_half, p_normed = sem("p_ready"), sem("inv_ready"), sem("mix_half"), sem("p_normed")
        p_turned, pt_ready, pv_done = sem("p_turned"), sem("pt_ready"), sem("pv_done")
        na_bias_ready, da_bias_ready = sem("na_bias_ready"), sem("da_bias_ready")
        o_hi_ready, o_lo_ready = sem("o_hi_ready"), sem("o_lo_ready")
        gate_exp, gate_den, gate_ready = sem("gate_exp"), sem("gate_den"), sem("gate_ready")
        m_parts, m_ready, m_hi_ready, m_lo_ready = sem("m_parts"), sem("m_ready"), sem("m_hi_ready"), sem("m_lo_ready")
        h2_ready, sq2_ready, sq2_used = sem("h2_ready"), sem("sq2_ready"), sem("sq2_used")
        q_ready, ps_ready, ssb_ready = sem("q_ready"), sem("ps_ready"), sem("ssb_ready")
        top_step, best_step, decode_step = sem("top_step"), sem("best_step"), sem("decode_step")
        g_exp_ready, g_inv_ready, routed = sem("g_exp_ready"), sem("g_inv_ready"), sem("routed")
        route_turned, route_ready, route_t_ready = sem("route_turned"), sem("route_ready"), sem("route_t_ready")
        seeded, acc_ready = sem("seeded"), sem("acc_ready")
        hot1_ready, hot2_ready, hot2_last = sem("hot1_ready"), sem("hot2_ready"), sem("hot2_last")
        hot_sq_ready = sem("hot_sq_ready")
        table_done, table_ready, table_scaled = sem("table_done"), sem("table_ready"), sem("table_scaled")
        up_low, up_summed = sem("up_low"), sem("up_summed")
        gelu_ready, pf_ready = sem("gelu_ready"), sem("pf_ready")
        p_hi_ready, p_lo_ready = sem("p_hi_ready"), sem("p_lo_ready")
        spare_done, spare_added = sem("spare_done"), sem("spare_added")
        out_ready, out3_ready, stored = sem("out_ready"), sem("out3_ready"), sem("stored")

        def load_chunk_a(sp, h, j, src, first=False):
            if not first:
                sp.wait_ge(chunk_used, CHUNKS_A * h + j - RING_A + 1)
            sp.dma_start(chunk_raw[j % RING_A][:], src).then_inc(landed[j % RING_A], 16)

        def load_chunk(sp, quad, slot, src):
            sp.wait_ge(chunk_used, 4 * quad + slot - RING + 1)
            sp.dma_start(chunk_raw[slot][:], src).then_inc(landed[slot], 16)

        def wait_alone(eng, semaphore, value):
            eng.wait_ge(semaphore, value)
            eng.nop(nofuse=True)

        def split_hi_a(act, h, j):
            act.wait_ge(landed[j % RING_A], 16 * (CHUNKS_A // RING_A * h + j // RING_A + 1))
            act.activation(chunk_hi[j % RING_A][:], chunk_raw[j % RING_A][:], ACT.Copy).then_inc(hi_ready, 1)

        def split_hi(act, quad, slot):
            act.wait_ge(landed[slot], 16 * (quad + 1 - BASE_B // RING + BASE_B // RING_A))
            act.activation(chunk_hi[slot][:], chunk_raw[slot][:], ACT.Copy).then_inc(hi_ready, 1)

        def split_lo_at(dve, number, slot):
            dve.wait_ge(hi_ready, number + 1)
            dve.tensor_tensor(chunk_lo[slot][:], chunk_raw[slot][:], chunk_hi[slot][:].bitcast(F32),
                              ALU.subtract).then_inc(lo_ready, 1)

        def split_lo(dve, quad, slot):
            split_lo_at(dve, 4 * quad + slot, slot)

        def step(split, eng, quad, j):
            split(eng, quad + (j + AHEAD) // RING, (j + AHEAD) % RING)

        def products(pe, number, slot, outp, rhs_hi, rhs_lo, kc0, n, start, stop):
            pe.wait_ge(lo_ready, number + 1)
            for k in range(8):
                w_hi = chunk_hi[slot][:, k * P:(k + 1) * P]
                w_lo = chunk_lo[slot][:, k * P:(k + 1) * P]
                r_hi, r_lo = rhs_hi[:, kc0 + k, 0:n], rhs_lo[:, kc0 + k, 0:n]
                pe.matmul(outp, w_hi, r_lo, start=start and k == 0, stop=False)
                pe.matmul(outp, w_lo, r_hi, start=False, stop=False)
                last = pe.matmul(outp, w_hi, r_hi, start=False, stop=stop and k == 7)
            last.then_inc(chunk_used, 1)

        def choices(r, h):
            return route[:, r, :, bass.ds(h * TOPK, TOPK)]

        def low_rows(eng, g, src, n, before, done):
            eng.wait_ge(x_hi_ready, before + g + 1)
            eng.tensor_tensor(x_lo[:, 4 * g:4 * g + 4, 0:n], src[:, 4 * g:4 * g + 4, :],
                              x_hi[:, 4 * g:4 * g + 4, 0:n].bitcast(F32), ALU.subtract).then_inc(done, 1)

        QV = BASE_V // 4
        Q0 = QV - EARLY // 2
        DVE_ROWS = 2
        NORMS = 5
        NORM_BLOCK = {0: 0, 1: 1, 2: 3, 3: 4}
        NORM_COLS = (T, L, T, L, T)
        block = ctx.enter_context(nc.Block())

        @block.sync
        def _(sp):
            sp.dma_start(ones[:], ones_d).then_inc(ones_in, 16)
            for g in range(4):
                sp.dma_start(h_t[:, 4 * g:4 * g + 4, :], h_turned[:, 4 * g:4 * g + 4, :]).then_inc(h_in[g], 16)
            sp.dma_start(gain[:], gains).then_inc(gain_in, 16)
            for j in range(2):
                load_chunk_a(sp, 0, j, w_in[j], first=True)
            for dst, src in ((pair_ones, pair_ones_d), (ident, ident_d), (da_bias, alibi), (iota, iota_d), (mask, na_mask)):
                sp.dma_start(dst[:], src).then_inc(const_in, 16)
            sp.dma_start(lam_v[:], lambdas).then_inc(lam_in, 16)
            for j in range(2, CHUNKS_A):
                load_chunk_a(sp, 0, j, w_in[j], first=j < RING_A)
            with sp.Fori(1, HEADS) as h:
                for j in range(CHUNKS_A):
                    load_chunk_a(sp, h, j, w_in[CHUNKS_A * h + j])
            for base, src in ((BASE_B, w_branch), (BASE_C, w_out)):
                with sp.Fori(0, HEADS) as i:
                    for j in range(4):
                        load_chunk(sp, base // 4 + i, j, src[4 * i + j])
                if base == BASE_C:
                    sp.wait_ge(chunk_used, BASE_C)
                    sp.dma_start(subk[:], sub_keys).then_inc(subk_in, 16)
            with sp.Fori(0, HEADS // 2) as i:
                for r in range(2):
                    for j in range(6):
                        n = 6 * r + j
                        src = w_query[8 * i + 4 * r + j] if j < 4 else peer_u[4 * i + 2 * r + j - 4]
                        load_chunk(sp, BASE_D // 4 + 3 * i + n // 4, n % 4, src)
            for j in range(4):
                load_chunk(sp, QV - 1, j, peer_u[2 * HEADS + j])
            for j in range(2):
                load_chunk(sp, QV, j, peer_v[0, j])
            with sp.Fori(0, EARLY // 2 - 1) as i:
                for j in range(2):
                    if j == 1:
                        sp.wait_ge(table_done, T)
                    load_chunk(sp, QV + i, 2 + j, peer_v[2 * i + 1, j])
                for j in range(2):
                    load_chunk(sp, QV + 1 + i, j, peer_v[2 * i + 2, j])
            with sp.Fori(EARLY, P) as b:
                for j in range(2):
                    load_chunk(sp, Q0 - 1 + b, 2 + j, peer_u[2 * b + j])
                for j in range(2):
                    load_chunk(sp, Q0 + b, j, peer_v[b - 1, j])
            for j in range(2):
                load_chunk(sp, N_CHUNKS // 4 - 1, 2 + j, peer_v[P - 1, j])
            for k, ready, count in ((0, out_ready, 1), (1, out_ready, 2), (4, out_ready, 3), (5, out_ready, 4),
                                    (6, spare_added, 2 * P - 1), (2, out_ready, 5), (7, spare_added, 2 * P),
                                    (3, out3_ready, 1)):
                sp.wait_ge(ready, count)
                src = out_sb[:, k, :] if k < 6 else acc[:, k - 6, :]
                sp.dma_start(out[(k // 4) * P:(k // 4 + 1) * P, (k % 4) * 512:(k % 4 + 1) * 512],
                             src).then_inc(stored, 16)
            sp.wait_ge(stored, 8 * 16)

        @block.gpsimd
        def _(pool):
            def load_rpb(h, par):
                for hh in range(2):
                    for tt in range(TT):
                        for half in range(2):
                            r = 2 * tt + half
                            src = skewed(rpb[h, hh, 7 - r, 0, GRID_W - 1:GRID_W])
                            pool.dma_start(rpb_t[half * GRID_W:(half + 1) * GRID_W, par, 2 * tt + hh, :]
                                           .rearrange("p (a b) -> p a b", a=ROWS), src).then_inc(rpb_in[par], 16)

            def skewed(first):
                return bass.AP(tensor=first.tensor, offset=first.offset,
                               ap=[[RPB_PITCH - 1, GRID_W], [GRID_W * RPB_PITCH, ROWS], [1, GRID_W]])

            def bias(h, par, rounds):
                pool.wait_ge(rpb_in[par], 128 * rounds)
                for u in range(4):
                    pool.tensor_tensor(na_bias[:, u, 0:T], rpb_t[:, par, u, :], mask[:], ALU.add) \
                        .then_inc(na_bias_ready, 1)

            low_rows(pool, 0, xf, L, 0, x_lo_pool)
            low_rows(pool, 2, xf, L, 0, x_lo_pool)
            load_rpb(0, 0)
            load_rpb(1, 1)
            pool.wait_ge(lam_dots, 2)
            pool.wait_ge(const_in, 5 * 16)
            pool.memset(na_bias[:, :, T:L], 0.0).then_inc(na_bias_ready, 1)
            bias(0, 0, 1)
            pool.wait_ge(max_ready, 4)
            pool.tensor_scalar(da_bias[:], da_bias[:], 0.5, None, ALU.mult).then_inc(da_bias_ready, 1)

            def rest(h, par, rounds, more):
                pool.wait_ge(max_ready, 8 * h)
                bias(h, par, rounds)
                if not more:
                    return
                load_rpb(h + 1, 1 - par)
                wait_alone(pool, max_ready, 8 * h + 4)
                pool.tensor_scalar(da_bias[:], da_bias[:], 0.5, None, ALU.mult).then_inc(da_bias_ready, 1)

            with pool.Fori(0, 3) as i:
                rest(2 * i + 1, 1, i + 1, True)
                rest(2 * i + 2, 0, i + 2, True)
            rest(HEADS - 1, 1, 4, False)

            low_rows(pool, 0, x2f, T, 4, x_lo_pool)
            low_rows(pool, 2, x2f, T, 4, x_lo_pool)

            pool.wait_ge(lo_ready, BASE_D + AHEAD)
            with pool.Fori(0, HEADS // 2) as i:
                for j in range(12):
                    step(split_lo, pool, BASE_D // 4 + 3 * i, j)
            for j in range(4):
                step(split_lo, pool, QV - 1, j)

        @block.scalar
        def _(act):
            act.preload_act_table_set("natural_log_exp_and_others")
            for g in range(4):
                act.wait_ge(h_in[g], 16)
                act.activation(sq_big[:, 4 * g:4 * g + 4, :], h_t[:, 4 * g:4 * g + 4, :], ACT.Square) \
                    .then_inc(sq_ready, 1)
            split_hi_a(act, 0, 0)
            act.wait_ge(consts_set, 2)
            act.wait_ge(ms_ready, 1)
            act.activation(ln_r[:], ms[:, 0:L], ACT.Ln, scale=1.0 / D, bias=eps[:]).then_inc(ln_ready, 1)
            act.wait_ge(ln_ready, 1)
            act.activation(rstd[:], ln_r[:], ACT.Exp, scale=-0.5).then_inc(r_ready, 1)
            for g in range(4):
                act.wait_ge(xf_ready, g + 1)
                act.activation(x_hi[:, 4 * g:4 * g + 4, :], xf[:, 4 * g:4 * g + 4, :], ACT.Copy).then_inc(x_hi_ready, 1)
                if g == 0:
                    split_hi_a(act, 0, 1)
            split_hi_a(act, 0, 2)
            act.wait_ge(lam_dots, 2)
            act.activation(lam_e[:], lam_e[:], ACT.Exp).then_inc(lam_exp, 1)

            def head(h, first):
                def square(i):
                    n = NORM_COLS[i]
                    src = att if i == 4 else blk[NORM_BLOCK[i] % 2]
                    if i == 4:
                        act.wait_ge(pv_done, 3 * h + 1)
                    else:
                        act.wait_ge(chunk_used, CHUNKS_A * h + 2 * NORM_BLOCK[i] + 2)
                    act.activation(sq[:, 0:n], src[:, 0:n], ACT.Square).then_inc(sq_ready, 1)

                def rsqrt(i, width):
                    n = NORM_COLS[i]
                    act.wait_ge(ms_ready, NORMS * h + i + 2)
                    act.activation(ln_r[:, 0:n], ms[:, 0:n], ACT.Ln, scale=1.0 / width, bias=eps[:]) \
                        .then_inc(ln_ready, 1)
                    act.wait_ge(ln_ready, NORMS * h + i + 2)
                    if not (first and i == 0):
                        act.wait_ge(normed, NORMS * h + i)
                    act.activation(rstd[:, 0:n], ln_r[:, 0:n], ACT.Exp, scale=-0.5).then_inc(r_ready, 1)

                def copy_v(i):
                    act.wait_ge(chunk_used, CHUNKS_A * h + (6 if i == 0 else 12))
                    if not (first and i == 0):
                        act.wait_ge(v_turned, 2 * h + i)
                    act.activation(v_t[:], blk[0 if i == 0 else 1][:, 0:L], ACT.Copy).then_inc(vt_ready, 1)

                def exp_units(u0):
                    act.wait_ge(t_ready, 4 * h + u0 // 2 + 1)
                    buf = t_da if u0 < 4 else t_na
                    for u in (u0, u0 + 1):
                        act.activation(buf[:, u % 4, :], buf[:, u % 4, :], ACT.Exp, bias=stat_neg[:, u:u + 1],
                                       accum_out=stat_sum[:, u:u + 1]).then_inc(p_ready, 1)

                def gate(k):
                    act.wait_ge(chunk_used, CHUNKS_A * h + 14 + 2 * k)
                    if not (first and k == 0):
                        act.wait_ge(gate_ready, 4 * h + k)
                    act.activation(gate_e[:], blk[k % 2][:, 0:T], ACT.Exp, scale=-1.0).then_inc(gate_exp, 1)

                def copy_turned(i):
                    act.wait_ge(p_turned, 3 * h + i + 1)
                    if not first:
                        act.wait_ge(pv_done, 3 * h - 2 + i)
                    act.activation(p_t[:, i, :, :].rearrange("p a b -> p (a b)"), turn[:], ACT.Copy) \
                        .then_inc(pt_ready, 1)
                    act.activation(p_meta[:, i, :], turn_m[0:META, 0:T], ACT.Copy).then_inc(pt_ready, 1)

                def tick(j):
                    split_hi_a(act, h, j + AHEAD)

                tick(0); tick(1); tick(2); square(0); tick(3); rsqrt(0, DH)
                tick(4); square(1); tick(5); rsqrt(1, DH)
                tick(6); copy_v(0); tick(7); exp_units(0)
                tick(8); exp_units(2); square(2); tick(9); rsqrt(2, DH)
                tick(10); copy_turned(0); square(3); tick(11); rsqrt(3, DH)
                tick(12); copy_v(1); square(4); tick(13); rsqrt(4, P)
                exp_units(4)
                tick(14); gate(0)
                act.wait_ge(normed, NORMS * h + 5)
                act.activation(o_hi[:, h, :], o_f[:], ACT.Copy).then_inc(o_hi_ready, 1)
                tick(15); exp_units(6)
                tick(16); gate(1); copy_turned(1)
                tick(17); copy_turned(2)
                tick(18); gate(2); tick(19)
                act.wait_ge(pv_done, 3 * h + 3)
                act.activation(o_hi[:, HEADS + h, :], att[:, 0:T], ACT.Copy).then_inc(o_hi_ready, 1)
                gate(3)

            head(0, True)
            with act.Fori(1, HEADS) as h:
                head(h, False)

            with act.Fori(0, HEADS) as i:
                for j in range(4):
                    if j % 2 == 1:
                        act.wait_ge(m_ready, 2 * i + j // 2 + 1)
                        act.activation(m_hi[:, 2 * i + j // 2, :], m_f[:, j // 2, :], ACT.Copy).then_inc(m_hi_ready, 1)
                    step(split_hi, act, BASE_B // 4 + i, j)

            def out_rows(i, first):
                for j in range(4):
                    if j % 2 == 1:
                        act.wait_ge(h2_ready, 2 * i + j // 2 + 1)
                        if not first:
                            act.wait_ge(sq2_used, 2 * i + j // 2 - 1)
                        act.activation(sq2[:, j // 2, :], h_t[:, 2 * i + j // 2, 0:T], ACT.Square).then_inc(sq2_ready, 1)
                    step(split_hi, act, BASE_C // 4 + i, j)
            out_rows(0, True)
            with act.Fori(1, HEADS) as i:
                out_rows(i, False)

            act.wait_ge(sq2_used, KC)
            act.activation(ln_r2[:], ms[:, 0:T], ACT.Ln, scale=1.0 / D, bias=eps[:]).then_inc(ln_ready, 1)
            act.wait_ge(ln_ready, NORMS * HEADS + 2)
            act.activation(rstd2[:], ln_r2[:], ACT.Exp, scale=-0.5).then_inc(r_ready, 1)
            for g in range(4):
                act.wait_ge(xf_ready, 4 + g + 1)
                act.activation(x_hi[:, 4 * g:4 * g + 4, 0:T], x2f[:, 4 * g:4 * g + 4, :], ACT.Copy) \
                    .then_inc(x_hi_ready, 1)

            for k in range(2):
                act.wait_ge(seeded, 2 + k)
                act.activation(acc[:, k, :], bank[6 + k][:], ACT.Copy).then_inc(acc_ready, 1)

            def gelu_early(b, used):
                act.wait_ge(chunk_used, used)
                act.activation(w2[:, b, :], up[:, 0:T], ACT.Gelu_apprx_tanh).then_inc(gelu_ready, 1)

            def route_head(i, r, first):
                h, base = 2 * i + r, BASE_D + 12 * i + 6 * r
                for j in range(6):
                    if j in (1, 3):
                        act.wait_ge(chunk_used, base + j + 1)
                        act.activation(q_sb[:, j // 2, :], blk[j // 2][:, 0:T], ACT.Copy).then_inc(q_ready, 1)
                    elif j == 4:
                        if not first:
                            act.wait_ge(routed, 2 * h - 2)
                        for p in range(2):
                            act.wait_ge(ps_ready, 2 * h + p + 1)
                            act.activation(s_sb[:, r, p::2, :], sc[p][:, 0:T].rearrange("p (a b) -> p a b", a=TT), ACT.Copy) \
                                .then_inc(ssb_ready, 1)
                    elif j == 5:
                        gelu_early(h, base + 6)
                    step(split_hi, act, BASE_D // 4 + 3 * i, 6 * r + j)
            route_head(0, 0, True)
            route_head(0, 1, True)
            with act.Fori(1, HEADS // 2) as i:
                route_head(i, 0, False)
                route_head(i, 1, False)
            for j in range(4):
                if j % 2 == 1:
                    gelu_early(HEADS + j // 2, BASE_V - 4 + j + 1)
                step(split_hi, act, QV - 1, j)

            act.wait_ge(route_ready, HEADS)
            act.activation(route[:, 2, :, :], route[:, 2, :, :], ACT.Exp).then_inc(g_exp_ready, 1)
            act.preload_act_table_set("gelu_apprx_tanh_and_others")
            for r in range(2):
                act.wait_ge(route_turned, r + 1)
                act.activation(route_t[:, r, :], turned[r], ACT.Copy).then_inc(route_t_ready, 1)

            def hot2_last_rows(i, par, first=False):
                if not first:
                    act.wait_ge(hot2_last, i)
                n = 4 - DVE_ROWS
                for k in range(n):
                    ins = act.activation(hot_sq[:, k, :], iota[:], ACT.Square, scale=-1.0,
                                         bias=route_t[:, 1, bass.ds(4 * i + 4 - n + k, 1)])
                ins.then_inc(hot_sq_ready, 1)
                act.wait_ge(hot_sq_ready, i + 1)
                act.activation(hot2[:, par, 4 - n:4, :], hot_sq[:, 0:n, :], ACT.Relu, scale=-1.0,
                               bias=one[:]).then_inc(hot2_last, 1)

            def table_out(i, k):
                act.wait_ge(table_scaled, i + 1)
                act.activation(w2[:, EARLY:P, bass.ds(4 * i, 4)],
                               bank[6 + k][:].rearrange("p (t e) -> p e t", t=4)[:, EARLY:P, :],
                               ACT.Copy).then_inc(table_ready, 1)

            def table_round(i, k):
                act.wait_ge(table_done, 4 * i - 4)
                hot2_last_rows(i, k)
                table_out(i - 2, k)

            act.wait_ge(route_t_ready, 3)
            hot2_last_rows(0, 0, True)
            hot2_last_rows(1, 1)
            with act.Fori(1, T // 8) as i:
                table_round(2 * i, 0)
                table_round(2 * i + 1, 1)
            table_out(T // 4 - 2, 0)
            table_out(T // 4 - 1, 1)

            def p_high(b, par):
                act.activation(p_hi[:, par, :], w2[:, b, :], ACT.Copy).then_inc(p_hi_ready, 1)

            act.wait_ge(table_scaled, T // 4)
            p_high(0, 0)
            p_high(1, 1)
            split_hi(act, QV, 3)

            def early(b, par, quad, slot):
                act.wait_ge(chunk_used, BASE_V + 2 * b)
                p_high(b + 1, 1 - par)
                split_hi(act, quad, slot)
                split_hi(act, quad, slot + 1)
            with act.Fori(0, EARLY // 2 - 1) as i:
                early(2 * i + 1, 1, QV + 1 + i, 0)
                early(2 * i + 2, 0, QV + 1 + i, 2)

            def round_(b, par):
                split_hi(act, Q0 + b, 0)
                split_hi(act, Q0 + b, 1)
                act.wait_ge(chunk_used, 4 * Q0 + 4 * b)
                act.activation(gelu[:], up[:, T:2 * T], ACT.Copy).then_inc(up_low, 1)
                split_hi(act, Q0 + b, 2)
                act.wait_ge(up_summed, b + 1 - EARLY)
                act.activation(gelu[:], gelu[:], ACT.Gelu_apprx_tanh).then_inc(gelu_ready, 1)
                split_hi(act, Q0 + b, 3)
                act.wait_ge(pf_ready, b + 1 - EARLY)
                act.activation(p_hi[:, par, :], p_f[:], ACT.Copy).then_inc(p_hi_ready, 1)
            with act.Fori(EARLY // 2, P // 2) as i:
                round_(2 * i, 0)
                round_(2 * i + 1, 1)

            act.wait_ge(chunk_used, N_CHUNKS - 1)
            for k in (0, 1, 4, 5):
                act.activation(out_sb[:, k, :], held[k][:], ACT.Copy).then_inc(out_ready, 1)
            act.wait_ge(chunk_used, N_CHUNKS)
            act.activation(out_sb[:, 2, :], held[2][:], ACT.Copy).then_inc(out_ready, 1)

        @block.vector
        def _(dve):
            dve.memset(eps[:], EPS).then_inc(consts_set, 1)
            dve.memset(one[:], 1.0).then_inc(consts_set, 1)
            split_lo_at(dve, 0, 0)
            dve.wait_ge(gain_in, 16)
            dve.wait_ge(r_ready, 1)

            def norm_rows(g, dst, src, n, col, rs):
                for kc in range(4 * g, 4 * g + 4):
                    ins = dve.scalar_tensor_tensor(dst[:, kc, :], src[:, kc, 0:n], gain[:, col + kc:col + kc + 1], rs[:],
                                                   ALU.mult, ALU.mult)
                ins.then_inc(xf_ready, 1)

            norm_rows(0, xf, h_t, L, G1, rstd)
            norm_rows(1, xf, h_t, L, G1, rstd)
            split_lo_at(dve, 1, 1)
            low_rows(dve, 1, xf, L, 0, x_lo_ready)
            norm_rows(2, xf, h_t, L, G1, rstd)
            norm_rows(3, xf, h_t, L, G1, rstd)
            low_rows(dve, 3, xf, L, 0, x_lo_ready)
            split_lo_at(dve, 2, 2)
            dve.wait_ge(lam_in, 16)
            for k in range(2):
                dve.tensor_tensor_reduce(lam_w[:], lam_v[:, 2 * k, :], lam_v[:, 2 * k + 1, :], 1.0, 0.0,
                                         ALU.mult, ALU.add, lam_e[:, k:k + 1]).then_inc(lam_dots, 1)
                dve.wait_ge(lam_dots, k + 1)
            dve.wait_ge(lam_exp, 1)
            dve.scalar_tensor_tensor(neg_lam[:], lam_e[:, 1:2], -LAM_INIT, lam_e[:, 0:1], ALU.add, ALU.subtract) \
                .then_inc(lam_done, 1)
            dve.tensor_scalar(gain[:, GQD:GQD + 1], gain[:, GQD:GQD + 1], DH ** -0.5, None, ALU.mult).then_inc(lam_step, 1)
            dve.tensor_scalar(gain[:, GQN:GQN + 1], gain[:, GQN:GQN + 1], DH ** -0.5, None, ALU.mult).then_inc(lam_step, 1)
            dve.tensor_scalar(gain[:, GOD:GOD + 1], gain[:, GOD:GOD + 1], 1.0 - LAM_INIT, None, ALU.mult).then_inc(lam_step, 1)
            dve.wait_ge(lam_step, 3)
            dve.wait_ge(lam_done, 1)
            dve.wait_ge(const_in, 5 * 16)

            def head(h, first):
                def scale(i):
                    dve.wait_ge(r_ready, NORMS * h + i + 2)
                    col = (GQD, GKD, GQN, GKN)[i]
                    n = NORM_COLS[i]
                    dve.scalar_tensor_tensor(qk[:, i, 0:n], blk[NORM_BLOCK[i] % 2][:, 0:n], gain[:, col:col + 1],
                                             rstd[:, 0:n], ALU.mult, ALU.mult).then_inc(normed, 1)

                def v_rows(i):
                    dve.wait_ge(v_turned, 2 * h + i + 1)
                    if not first:
                        dve.wait_ge(pv_done, 3 * h - (2 if i == 0 else 0))
                    dve.tensor_copy(v_tok[:, i, :, :].rearrange("p a b -> p (a b)"), turn[:, 0:2 * P]).then_inc(v_ready, 1)
                    dve.tensor_copy(v_meta[:, i, :], turn_m[0:META, 0:P]).then_inc(v_ready, 1)

                def maxima(u0):
                    buf = t_da if u0 < 4 else t_na
                    for u in (u0, u0 + 1):
                        wait_alone(dve, s_ready, 8 * h + u + 1)
                        bias = da_bias[:, u // 2, :] if u < 4 else na_bias[:, u % 4, :]
                        dve.tensor_tensor_reduce(buf[:, u % 4, :], sc[u % 2][:, 0:L], bias, 1.0, MASKED,
                                                 ALU.add, ALU.max, stat_max[:, u:u + 1]).then_inc(max_ready, 1)
                    dve.wait_ge(max_ready, 8 * h + u0 + 2)
                    dve.tensor_scalar(stat_neg[:, u0:u0 + 2], stat_max[:, u0:u0 + 2], -1.0, None, ALU.mult) \
                        .then_inc(t_ready, 1)

                def gate(k):
                    dve.wait_ge(gate_exp, 4 * h + k + 1)
                    dve.tensor_scalar(gate_e[:], gate_e[:], 1.0, None, ALU.add).then_inc(gate_den, 1)
                    dve.wait_ge(gate_den, 4 * h + k + 1)
                    dve.reciprocal(gates[:, (k // 2) * KC + 2 * h + k % 2, :], gate_e[:]).then_inc(gate_ready, 1)

                def mix_da():
                    dve.wait_ge(p_ready, 8 * h + 4)
                    dve.reciprocal(stat_inv[:, 0:4], stat_sum[:, 0:4]).then_inc(inv_ready, 1)
                    dve.wait_ge(inv_ready, 2 * h + 1)
                    for tt in range(TT):
                        dve.tensor_scalar(t_da[:, 2 * tt + 1, :], t_da[:, 2 * tt + 1, :],
                                          stat_inv[:, 2 * tt + 1:2 * tt + 2], neg_lam[:], ALU.mult, ALU.mult) \
                            .then_inc(mix_half, 1)
                    for tt in range(TT):
                        dve.wait_ge(mix_half, 2 * h + tt + 1)
                        ins = dve.scalar_tensor_tensor(t_da[:, 2 * tt, :], t_da[:, 2 * tt, :],
                                                       stat_inv[:, 2 * tt:2 * tt + 1], t_da[:, 2 * tt + 1, :],
                                                       ALU.mult, ALU.add)
                        ins.then_inc(p_normed, 1)

                def norm_na():
                    dve.wait_ge(p_ready, 8 * h + 8)
                    dve.reciprocal(stat_inv[:, 4:8], stat_sum[:, 4:8]).then_inc(inv_ready, 1)
                    dve.wait_ge(inv_ready, 2 * h + 2)
                    for u in (0, 2, 1, 3):
                        dve.tensor_scalar(t_na[:, u, :], t_na[:, u, :], stat_inv[:, 4 + u:5 + u], None, ALU.mult) \
                            .then_inc(p_normed, 1)

                def tick(j):
                    split_lo_at(dve, CHUNKS_A * h + j + AHEAD, (j + AHEAD) % RING_A)

                tick(0); tick(1); tick(2)
                if not first:
                    dve.wait_ge(p_turned, 3 * h)
                    dve.wait_ge(da_bias_ready, h)
                tick(3); scale(0)
                tick(4); tick(5); scale(1)
                tick(6); v_rows(0); maxima(0)
                tick(7); maxima(2)
                tick(8); mix_da(); tick(9); scale(2)
                tick(10); tick(11); scale(3)
                tick(12); v_rows(1)
                dve.wait_ge(na_bias_ready, 1 + 4 * (h + 1))
                maxima(4)
                tick(13)
                dve.wait_ge(r_ready, NORMS * h + 6)
                if not first:
                    dve.wait_ge(o_hi_ready, 2 * h)
                dve.scalar_tensor_tensor(o_f[:], att[:, 0:T], gain[:, GOD:GOD + 1], rstd[:, 0:T],
                                         ALU.mult, ALU.mult).then_inc(normed, 1)
                maxima(6)
                tick(14); gate(0)
                dve.wait_ge(o_hi_ready, 2 * h + 1)
                dve.tensor_tensor(o_lo[:, h, :], o_f[:], o_hi[:, h, :].bitcast(F32), ALU.subtract).then_inc(o_lo_ready, 1)
                tick(15); norm_na()
                tick(16); gate(1); tick(17)
                tick(18); gate(2); tick(19)
                dve.wait_ge(o_hi_ready, 2 * h + 2)
                dve.tensor_tensor(o_lo[:, HEADS + h, :], att[:, 0:T], o_hi[:, HEADS + h, :].bitcast(F32),
                                  ALU.subtract).then_inc(o_lo_ready, 1)
                gate(3)

            head(0, True)
            with dve.Fori(1, HEADS) as h:
                head(h, False)

            with dve.Fori(0, HEADS) as i:
                for j in range(4):
                    if j % 2 == 1:
                        k = j // 2
                        dve.wait_ge(chunk_used, BASE_B + 4 * i + 2 * k + 2)
                        yd, yn = (blk, sc)[k]
                        dve.tensor_tensor(m_a[:, k, :], yd[:, 0:T], gates[:, 2 * i + k, :], ALU.mult).then_inc(m_parts, 1)
                        dve.tensor_tensor(m_b[:, k, :], yn[:, 0:T], gates[:, KC + 2 * i + k, :], ALU.mult).then_inc(m_parts, 1)
                        dve.wait_ge(m_parts, 4 * i + 2 * k + 2)
                        dve.tensor_tensor(m_f[:, k, :], m_a[:, k, :], m_b[:, k, :], ALU.add).then_inc(m_ready, 1)
                        dve.wait_ge(m_hi_ready, 2 * i + k + 1)
                        dve.tensor_tensor(m_lo[:, 2 * i + k, :], m_f[:, k, :], m_hi[:, 2 * i + k, :].bitcast(F32),
                                          ALU.subtract).then_inc(m_lo_ready, 1)
                    step(split_lo, dve, BASE_B // 4 + i, j)

            with dve.Fori(0, HEADS) as i:
                for j in range(4):
                    if j % 2 == 1:
                        k = j // 2
                        dve.wait_ge(chunk_used, BASE_C + 4 * i + 2 * k + 2)
                        dve.tensor_tensor(h_t[:, 2 * i + k, 0:T], blk[k][:, 0:T], h_t[:, 2 * i + k, 0:T], ALU.add) \
                            .then_inc(h2_ready, 1)
                    step(split_lo, dve, BASE_C // 4 + i, j)

            dve.wait_ge(r_ready, NORMS * HEADS + 2)
            dve.wait_ge(h2_ready, KC)
            norm_rows(0, x2f, h_t, T, G2, rstd2)
            norm_rows(1, x2f, h_t, T, G2, rstd2)
            norm_rows(2, x2f, h_t, T, G2, rstd2)
            low_rows(dve, 1, x2f, T, 4, x_lo_ready)
            norm_rows(3, x2f, h_t, T, G2, rstd2)
            low_rows(dve, 3, x2f, T, 4, x_lo_ready)

            def route_head(h, r):
                wait_alone(dve, ssb_ready, 2 * h + 2)
                lists = range(4)
                for n in lists:
                    dve.max(top[:, n, 0:8], s_sb[:, r, n, :]).then_inc(top_step, 1)
                for n in lists:
                    wait_alone(dve, top_step, 20 * h + n + 1)
                    dve.match_replace(s_rest[:, n, :], top[:, n, 0:8], s_sb[:, r, n, :], LOWEST).then_inc(top_step, 1)
                for n in lists:
                    wait_alone(dve, top_step, 20 * h + 4 + n + 1)
                    dve.max(top[:, n, 8:16], s_rest[:, n, :]).then_inc(top_step, 1)
                for n in lists:
                    dve.max_index(top_i[:, n, 0:8], top[:, n, 0:8], s_sb[:, r, n, :]).then_inc(top_step, 1)
                for n in lists:
                    wait_alone(dve, top_step, 20 * h + 8 + n + 1)
                    dve.max_index(top_i[:, n, 8:16], top[:, n, 8:16], s_rest[:, n, :]).then_inc(top_step, 1)
                dve.tensor_tensor(cand[:].rearrange("p t (a b) -> p t a b", a=TOPK),
                                  top[:, 0::2, :].unsqueeze(3).broadcast_to([P, TT, TOPK, TOPK]),
                                  top[:, 1::2, :].unsqueeze(2).broadcast_to([P, TT, TOPK, TOPK]),
                                  ALU.add).then_inc(best_step, 1)
                dve.wait_ge(top_step, 20 * h + 20)
                dve.tensor_copy(top_f[:], top_i[:]).then_inc(decode_step, 1)
                wait_alone(dve, best_step, 11 * h + 1)
                for tt in range(TT):
                    dve.max(best[:, tt, 0:8], cand[:, tt, :]).then_inc(best_step, 1)
                for tt in range(TT):
                    wait_alone(dve, best_step, 11 * h + 2 + tt)
                    dve.match_replace(cand_rest[:, tt, :], best[:, tt, 0:8], cand[:, tt, :], LOWEST).then_inc(best_step, 1)
                for tt in range(TT):
                    wait_alone(dve, best_step, 11 * h + 4 + tt)
                    dve.max(best[:, tt, 8:16], cand_rest[:, tt, :]).then_inc(best_step, 1)
                dve.wait_ge(best_step, 11 * h + 7)
                dve.tensor_tensor(choices(2, h), best[:], best[:, :, 0:1].broadcast_to([P, TT, TOPK]),
                                  ALU.subtract).then_inc(route_ready, 1)
                for tt in range(TT):
                    dve.max_index(best_i[:, tt, 0:8], best[:, tt, 0:8], cand[:, tt, :]).then_inc(best_step, 1)
                for tt in range(TT):
                    dve.max_index(best_i[:, tt, 8:16], best[:, tt, 8:16], cand_rest[:, tt, :]).then_inc(best_step, 1)
                dve.wait_ge(best_step, 11 * h + 11)
                dve.tensor_scalar(pos_i[:, :, 0, :], best_i[:], 4, None, ALU.logical_shift_right).then_inc(decode_step, 1)
                dve.tensor_scalar(pos_i[:, :, 1, :], best_i[:], 15, None, ALU.bitwise_and).then_inc(decode_step, 1)
                dve.wait_ge(decode_step, 6 * h + 3)
                dve.tensor_copy(pos_f[:], pos_i[:]).then_inc(decode_step, 1)
                dve.wait_ge(decode_step, 6 * h + 4)
                dve.tensor_tensor(eq[:], pos_f[:].rearrange("p t l k -> p (t l) k").unsqueeze(3)
                                  .broadcast_to([P, 4, TOPK, TOPK]),
                                  iota[:, 0:TOPK].unsqueeze(1).unsqueeze(1).broadcast_to([P, 4, TOPK, TOPK]),
                                  ALU.is_equal).then_inc(decode_step, 1)
                dve.wait_ge(decode_step, 6 * h + 5)
                dve.tensor_tensor(eqv[:], eq[:], top_f[:].unsqueeze(2).broadcast_to([P, 4, TOPK, TOPK]),
                                  ALU.mult).then_inc(decode_step, 1)
                dve.wait_ge(decode_step, 6 * h + 6)
                for l in range(2):
                    dve.tensor_reduce(choices(l, h), eqv[:, l::2, :, :], AX.X, ALU.add) \
                        .then_inc(routed, 1)
            with dve.Fori(0, HEADS // 2) as i:
                route_head(2 * i, 0)
                route_head(2 * i + 1, 1)

            by_head = route[:, 2, :, :].rearrange("p t (h k) -> p t h k", h=HEADS)
            dve.wait_ge(g_exp_ready, 1)
            dve.tensor_reduce(g_sum[:], by_head, AX.X, ALU.add).then_inc(g_inv_ready, 1)
            dve.wait_ge(g_inv_ready, 1)
            dve.reciprocal(g_inv[:], g_sum[:]).then_inc(g_inv_ready, 1)
            dve.wait_ge(g_inv_ready, 2)
            dve.tensor_tensor(by_head, by_head, g_inv[:].unsqueeze(3).broadcast_to([P, TT, HEADS, TOPK]),
                              ALU.mult).then_inc(route_ready, 1)

            dve.wait_ge(route_turned, 3)
            dve.tensor_copy(route_t[:, 2, :], turned[2]).then_inc(route_t_ready, 1)
            dve.wait_ge(route_t_ready, 3)

            def weigh_early(i, k):
                dve.wait_ge(table_done, 4 * i + 4)
                cells = w2[:, 0:EARLY, bass.ds(4 * i, 4)]
                dve.tensor_tensor(cells, bank[6 + k][:].rearrange("p (t e) -> p e t", t=4)[:, 0:EARLY, :], cells,
                                  ALU.mult).then_inc(table_scaled, 1)

            def hot_rows(i, par, first=False):
                if not first:
                    weigh_early(i - 2, par)
                for k in range(4):
                    t = 4 * i + k
                    dve.tensor_scalar(hot1[:, par, k, :], iota[:], route_t[:, 0, bass.ds(t, 1)],
                                      route_t[:, 2, bass.ds(t, 1)], ALU.is_equal, ALU.mult).then_inc(hot1_ready, 1)
                    if k < DVE_ROWS:
                        dve.tensor_scalar(hot2[:, par, k, :], iota[:], route_t[:, 1, bass.ds(t, 1)], None,
                                          ALU.is_equal).then_inc(hot2_ready, 1)
            hot_rows(0, 0, first=True)
            hot_rows(1, 1, first=True)
            with dve.Fori(1, T // 8) as i:
                hot_rows(2 * i, 0)
                hot_rows(2 * i + 1, 1)
            weigh_early(T // 4 - 2, 0)
            weigh_early(T // 4 - 1, 1)

            def p_low(b, par, src):
                dve.wait_ge(p_hi_ready, b + 1)
                dve.tensor_tensor(p_lo[:, par, :], src, p_hi[:, par, :].bitcast(F32), ALU.subtract).then_inc(p_lo_ready, 1)

            def add_spare(b, k, used=None):
                if k == 0:
                    dve.wait_ge(spare_done, b + 1)
                else:
                    dve.wait_ge(chunk_used, used)
                dve.tensor_tensor(acc[:, k, :], spare[:], acc[:, k, :], ALU.add).then_inc(spare_added, 1)

            dve.wait_ge(table_scaled, T // 4)
            dve.wait_ge(acc_ready, 2)
            p_low(0, 0, w2[:, 0, :])
            p_low(1, 1, w2[:, 1, :])
            dve.wait_ge(lo_ready, BASE_V + AHEAD)
            split_lo(dve, QV, 3)
            add_spare(0, 0)
            add_spare(0, 1, BASE_V + 2)

            def early(b, par, quad, slot):
                p_low(b + 1, 1 - par, w2[:, b + 1, :])
                split_lo(dve, quad, slot)
                add_spare(b, 0)
                split_lo(dve, quad, slot + 1)
                add_spare(b, 1, BASE_V + 2 * b + 2)
            with dve.Fori(0, EARLY // 2 - 1) as i:
                early(2 * i + 1, 1, QV + 1 + i, 0)
                early(2 * i + 2, 0, QV + 1 + i, 2)
            dve.wait_ge(table_ready, T // 4)

            def round_(b, par):
                split_lo(dve, Q0 + b, 0)
                split_lo(dve, Q0 + b, 1)
                dve.wait_ge(up_low, b + 1 - EARLY)
                dve.tensor_tensor(gelu[:], up[:, 0:T], gelu[:], ALU.add).then_inc(up_summed, 1)
                split_lo(dve, Q0 + b, 2)
                dve.wait_ge(gelu_ready, b + 1)
                dve.wait_ge(p_lo_ready, b)
                dve.tensor_tensor(p_f[:], gelu[:], w2[:, b, :], ALU.mult).then_inc(pf_ready, 1)
                add_spare(b - 1, 0)
                split_lo(dve, Q0 + b, 3)
                add_spare(b - 1, 1, 4 * Q0 + 4 * b + 2)
                p_low(b, par, p_f[:])
            with dve.Fori(EARLY // 2, P // 2) as i:
                round_(2 * i, 0)
                round_(2 * i + 1, 1)
            add_spare(P - 1, 0)
            add_spare(P - 1, 1, N_CHUNKS)
            dve.tensor_copy(out_sb[:, 3, :], held[3][:]).then_inc(out3_ready, 1)

        @block.tensor
        def _(pe):
            pe.wait_ge(ones_in, 16)
            for kc in range(KC):
                if kc % 4 == 0:
                    pe.wait_ge(sq_ready, kc // 4 + 1)
                ins = pe.matmul(ms[:, 0:L], ones[:], sq_big[:, kc, :], start=kc == 0, stop=kc == KC - 1)
            ins.then_inc(ms_ready, 1)
            pe.wait_ge(const_in, 5 * 16)

            def head(h, first):
                def chunk(c):
                    j, half = c // 2, c % 2
                    w = T if j in (0, 3) or j > 5 else L
                    if half == 0:
                        free_bank(j)
                    if first and c < 2:
                        pe.wait_ge(x_lo_ready, c + 1)
                        pe.wait_ge(x_lo_pool, c + 1)
                    products(pe, CHUNKS_A * h + c, c % RING_A, blk[j % 2][:, 0:w], x_hi, x_lo, 8 * half, w,
                             half == 0, half == 1)

                def free_bank(j):
                    if j < 2:
                        if not first:
                            pe.wait_ge(gate_exp, 4 * h - 1 + j)
                    elif j in (2, 3, 5, 6):
                        pe.wait_ge(normed, NORMS * h + {2: 1, 3: 2, 5: 3, 6: 4}[j])
                    elif j in (4, 7):
                        pe.wait_ge(vt_ready, 2 * h + (1 if j == 4 else 2))
                    else:
                        pe.wait_ge(gate_exp, 4 * h + j - 7)

                def mean_square(i):
                    w = NORM_COLS[i]
                    pe.wait_ge(sq_ready, NORMS * h + 4 + i + 1)
                    pe.matmul(ms[:, 0:w], (ones if i == 4 else pair_ones)[:], sq[:, 0:w], start=True, stop=True) \
                        .then_inc(ms_ready, 1)

                def turn_v(i):
                    pe.wait_ge(vt_ready, 2 * h + i + 1)
                    if i == 1:
                        pe.wait_ge(pt_ready, 6 * h + 2)
                    elif not first:
                        pe.wait_ge(pt_ready, 6 * h)
                    pe.transpose(turn[:, 0:P], v_t[:, 0:P], ident[:])
                    pe.transpose(turn[:, P:2 * P], v_t[:, P:2 * P], ident[:])
                    pe.transpose(turn_m[0:META, 0:P], v_t[:, T:L], ident[:]).then_inc(v_turned, 1)

                def score(u):
                    if u == 0:
                        pe.wait_ge(normed, NORMS * h + 2)
                    if u == 4:
                        pe.wait_ge(normed, NORMS * h + 4)
                    if not (first and u < 2):
                        pe.wait_ge(max_ready, 8 * h + u - 1)
                    q, k = (0, 1) if u < 4 else (2, 3)
                    half, tt = u % 2, (u % 4) // 2
                    rows = slice(half * DH, (half + 1) * DH)
                    pe.matmul(sc[u % 2][:, 0:L], qk[rows, q, tt * P:(tt + 1) * P], qk[rows, k, :],
                              start=True, stop=True).then_inc(s_ready, 1)

                def turn_p(i):
                    if i == 0:
                        pe.wait_ge(v_ready, 4 * h + 2)
                        pe.wait_ge(p_normed, 6 * h + 2)
                    elif i == 1:
                        pe.wait_ge(v_ready, 4 * h + 4)
                        pe.wait_ge(p_normed, 6 * h + 4)
                    else:
                        pe.wait_ge(pt_ready, 6 * h + 4)
                        pe.wait_ge(p_normed, 6 * h + 6)
                    for tt in range(TT):
                        src = t_da[:, 2 * tt, :] if i == 0 else t_na[:, 2 * tt + i - 1, :]
                        for kt in range(2):
                            pe.transpose(turn[:, kt * T + tt * P:kt * T + (tt + 1) * P], src[:, kt * P:(kt + 1) * P], ident[:])
                        ins = pe.transpose(turn_m[0:META, tt * P:(tt + 1) * P], src[:, T:L], ident[:])
                    ins.then_inc(p_turned, 1)

                def pv(i):
                    pe.wait_ge(pt_ready, 6 * h + 2 * i + 2)
                    if i == 0:
                        if not first:
                            pe.wait_ge(o_lo_ready, 2 * h)
                    elif i == 1:
                        pe.wait_ge(normed, NORMS * h + 5)
                    rows = slice(0, P) if i == 0 else slice((i - 1) * DH, i * DH)
                    n = 0 if i == 0 else 1
                    for kt in range(2):
                        pe.matmul(att[rows, 0:T], v_tok[:, n, kt, rows], p_t[:, i, kt, :], start=kt == 0, stop=False)
                    pe.matmul(att[rows, 0:T], v_meta[:, n, rows], p_meta[:, i, :], start=False, stop=True) \
                        .then_inc(pv_done, 1)

                chunk(0); chunk(1); chunk(2); mean_square(0)
                chunk(3); chunk(4); mean_square(1)
                chunk(5); chunk(6); turn_v(0); score(0); score(1)
                chunk(7); score(2); score(3)
                chunk(8); mean_square(2)
                chunk(9); turn_p(0)
                chunk(10); mean_square(3); pv(0)
                chunk(11); chunk(12); turn_v(1); mean_square(4); score(4); score(5)
                chunk(13); score(6); score(7)
                chunk(14); chunk(15); chunk(16); turn_p(1)
                chunk(17); turn_p(2); pv(1)
                chunk(18); pv(2)
                chunk(19)

            head(0, True)
            with pe.Fori(1, HEADS) as h:
                head(h, False)

            pe.wait_ge(max_ready, 8 * HEADS)

            def branch_rows(i, first):
                for k in range(2):
                    if not first:
                        pe.wait_ge(m_parts, 4 * i - 2 + 2 * k)
                    for j in range(2):
                        if first and k == 0:
                            pe.wait_ge(o_lo_ready, 2 * HEADS - 1 + j)
                            pe.wait_ge(gate_exp, 4 * HEADS - 1 + j)
                        products(pe, BASE_B + 4 * i + 2 * k + j, 2 * k + j, (blk, sc)[k][j][:, 0:T], o_hi, o_lo, j * HEADS, T,
                                 True, True)
            branch_rows(0, True)
            with pe.Fori(1, HEADS) as i:
                branch_rows(i, False)

            def out_rows(i, first, last):
                for k in range(2):
                    if not first:
                        pe.wait_ge(h2_ready, 2 * i + k - 1)
                    for s in range(2):
                        if first and k == 0:
                            pe.wait_ge(m_lo_ready, 8 * s + 8)
                        products(pe, BASE_C + 4 * i + 2 * k + s, 2 * k + s, blk[k][:, 0:T], m_hi, m_lo, 8 * s, T, s == 0, s == 1)
                    if k == 0 and first:
                        continue
                    square_sum(2 * i + k - 1, (k + 1) % 2, first, False)
                if last:
                    square_sum(2 * i + 1, 1, False, True)

            def square_sum(n, par, start, stop):
                pe.wait_ge(sq2_ready, n + 1)
                pe.matmul(ms[:, 0:T], ones[:], sq2[:, par, :], start=start, stop=stop).then_inc(sq2_used, 1)

            pe.wait_ge(m_parts, 4 * HEADS - 2)
            out_rows(0, True, False)
            with pe.Fori(1, HEADS - 1) as i:
                out_rows(i, False, False)
            out_rows(HEADS - 1, False, True)

            def seed(k, n_bank):
                tt, dc = k // 4, k % 4
                for n in range(4):
                    ins = pe.matmul(bank[n_bank][:, n * P:(n + 1) * P], h_t[:, 4 * dc + n, tt * P:(tt + 1) * P], ident[:],
                                    start=n == 0, stop=True, skip_group_check=True)
                ins.then_inc(seeded, 1)

            pe.wait_ge(h2_ready, KC)
            for k in (5, 6, 7):
                seed(k, k)
            pe.wait_ge(ln_ready, NORMS * HEADS + 2)
            seed(2, 2)

            pe.wait_ge(subk_in, 16)

            def up_rows(b, quad, slot, first=False, between=None):
                if not first:
                    pe.wait_ge(gelu_ready, b)
                for s in range(2):
                    products(pe, 4 * quad + slot + s, slot + s, up[:, 0:T], x_hi, x_lo, 8 * s, T, s == 0, s == 1)
                    if s == 0 and between:
                        between()

            def query_head(i, r, first):
                h = 2 * i + r
                for p in range(2):
                    if not first and p == 0:
                        pe.wait_ge(q_ready, 2 * h)
                    for s in range(2):
                        n = 6 * r + 2 * p + s
                        if first and p == 0:
                            pe.wait_ge(x_lo_ready, 2 + s + 1)
                            pe.wait_ge(x_lo_pool, 2 + s + 1)
                        products(pe, BASE_D + 12 * i + n, n % 4, blk[p][:, 0:T], x_hi, x_lo, 8 * s, T, s == 0, s == 1)

                def scores():
                    if not first:
                        pe.wait_ge(ssb_ready, 2 * h)
                    for p in range(2):
                        pe.wait_ge(q_ready, 2 * h + p + 1)
                        for tt in range(TT):
                            ins = pe.matmul(sc[p][:, tt * P:(tt + 1) * P], q_sb[:, p, tt * P:(tt + 1) * P], subk[:, p, :],
                                            start=True, stop=True)
                        ins.then_inc(ps_ready, 1)
                if first:
                    pe.wait_ge(acc_ready, 1)
                n = 6 * r + 4
                up_rows(h, BASE_D // 4 + 3 * i + n // 4, n % 4, first, scores)
            query_head(0, 0, True)
            query_head(0, 1, False)
            with pe.Fori(1, HEADS // 2) as i:
                query_head(i, 0, False)
                query_head(i, 1, False)
            for n in range(2):
                up_rows(HEADS + n, QV - 1, 2 * n)
            pe.wait_ge(q_ready, 2 * HEADS)
            pe.wait_ge(ssb_ready, 2 * HEADS)
            for k in (0, 1, 3, 4):
                seed(k, k)

            pe.wait_ge(routed, 2 * HEADS)
            pe.wait_ge(acc_ready, 2)
            pe.wait_ge(gelu_ready, EARLY)
            for r in range(3):
                if r == 2:
                    pe.wait_ge(route_ready, HEADS + 1)
                    pe.wait_ge(route_t_ready, 1)
                for tt in range(TT):
                    ins = pe.transpose(turned[r][:, tt * P:(tt + 1) * P], route[:, r, tt, :], ident[:])
                ins.then_inc(route_turned, 1)

            def table(i, k, first):
                if not first:
                    pe.wait_ge(table_ready, i - 1)
                for n in range(4):
                    pe.wait_ge(hot1_ready, 4 * i + n + 1)
                    if n < DVE_ROWS:
                        pe.wait_ge(hot2_ready, DVE_ROWS * i + n + 1)
                    elif n == DVE_ROWS:
                        pe.wait_ge(hot2_last, i + 1)
                    pe.matmul(bank[6 + k][:, n * P:(n + 1) * P], hot2[:, k, n, :], hot1[:, k, n, :], start=True, stop=True) \
                        .then_inc(table_done, 1)
            table(0, 0, True)
            table(1, 1, True)
            with pe.Fori(1, T // 8) as i:
                table(2 * i, 0, False)
                table(2 * i + 1, 1, False)

            def up_rows_paired(b, quad, slot):
                pe.wait_ge(gelu_ready, b)
                for s in range(2):
                    pe.wait_ge(lo_ready, 4 * quad + slot + s + 1)
                    for k in range(8):
                        cols = slice(k * P, (k + 1) * P)
                        first, last = s == 0 and k == 0, s == 1 and k == 7
                        pe.matmul(up[:], chunk_hi[slot + s][:, cols], x_parts[:, 8 * s + k, :, 0:T],
                                  start=first, stop=last, skip_group_check=True)
                        ins = pe.matmul(up[:, T:2 * T], chunk_lo[slot + s][:, cols], x_hi[:, 8 * s + k, 0:T],
                                        start=False, stop=last, skip_group_check=True)
                    ins.then_inc(chunk_used, 1)

            def down_tile(outp, tt, par, slot, dcl, start, stop):
                a_hi = p_hi[:, par, tt * P:(tt + 1) * P]
                a_lo = p_lo[:, par, tt * P:(tt + 1) * P]
                cols = slice(dcl * 512, (dcl + 1) * 512)
                pe.matmul(outp, a_hi, chunk_lo[slot][:, cols], start=start, stop=False, skip_group_check=True)
                pe.matmul(outp, a_lo, chunk_hi[slot][:, cols], start=False, stop=False, skip_group_check=True)
                return pe.matmul(outp, a_hi, chunk_hi[slot][:, cols], start=False, stop=stop, skip_group_check=True)

            def down_rows(b, par, quad, slot, first):
                pe.wait_ge(p_lo_ready, b + 1)
                pe.wait_ge(lo_ready, 4 * quad + slot + 1)
                for k in (0, 1, 4, 5):
                    ins = down_tile(held[k][:], k // 4, par, slot, k % 4, False, True)
                ins.then_inc(chunk_used, 1)
                slot += 1
                pe.wait_ge(lo_ready, 4 * quad + slot + 1)
                for n, k in enumerate((6, 2, 3, 7)):
                    if k >= 6:
                        if not (first and k == 6):
                            pe.wait_ge(spare_added, 2 * b + k - 6)
                        ins = down_tile(spare[:], 1, par, slot, k - 6, True, True)
                        if k == 6:
                            ins.then_inc(spare_done, 1)
                    else:
                        ins = down_tile(held[k][:], 0, par, slot, k - 2, False, True)
                ins.then_inc(chunk_used, 1)

            pe.wait_ge(table_ready, T // 4)
            down_rows(0, 0, QV, 0, True)
            with pe.Fori(0, EARLY // 2 - 1) as i:
                down_rows(2 * i + 1, 1, QV + i, 2, False)
                down_rows(2 * i + 2, 0, QV + 1 + i, 0, False)

            def round_(b, par_prev):
                up_rows_paired(b, Q0 - 1 + b, 2)
                down_rows(b - 1, par_prev, Q0 + b, 0, False)
            with pe.Fori(EARLY // 2, P // 2) as i:
                round_(2 * i, 1)
                round_(2 * i + 1, 0)
            down_rows(P - 1, 1, N_CHUNKS // 4 - 1, 2, False)


def kernel(**inputs):
    import concourse.bacc as bacc
    from concourse.bass_utils import run_bass_kernel_spmd

    f = {k: np.asarray(v) for k, v in inputs.items()}

    def by_block(w, kc):
        n = w.shape[1] // P
        return w.reshape(kc, P, n, P).transpose(2, 1, 0, 3)

    def chunks(w):
        n, _, kc, _ = w.shape
        return w.reshape(n, P, kc // 8, 8, P).transpose(0, 2, 1, 3, 4).reshape(n * kc // 8, P, CH)

    arrays = {}
    h = np.concatenate([f["x"][0], f["meta_tokens"]], axis=0)
    arrays["h_turned"] = h.reshape(L, KC, P).transpose(2, 1, 0)
    def twice(g):
        return np.concatenate([g[0], g[0]])[:, None]
    arrays["gains"] = np.concatenate(
        [f["norm1_g"][0].reshape(KC, P).T, f["norm2_g"][0].reshape(KC, P).T, twice(f["da_q_norm_g"]),
         twice(f["da_k_norm_g"]), twice(f["na_q_norm_g"]), twice(f["na_k_norm_g"]), f["da_out_norm_g"][0][:, None]], axis=1)
    arrays["lambdas"] = np.broadcast_to(
        np.stack([f["lambda_q1"][0], f["lambda_k1"][0], f["lambda_q2"][0], f["lambda_k2"][0]])[None], (P, 4, DH))
    q = (META + np.arange(T)).reshape(TT, P).T
    k = np.concatenate([META + np.arange(T), np.arange(META)])
    arrays["alibi"] = (-0.5 * np.abs(q[:, :, None] - k[None, None, :])).astype(np.float32)
    c = np.arange(P) % GRID_W
    first = np.clip(c - WIN_W // 2, 0, GRID_W - WIN_W)[:, None]
    kc_ = (np.arange(T) % GRID_W)[None]
    arrays["na_mask"] = np.where((kc_ >= first) & (kc_ < first + WIN_W), 0.0, MASKED).astype(np.float32)
    pad = np.zeros((2 * HEADS, RPB_H, RPB_PITCH), np.float32)
    pad[:, :, GRID_W - WIN_W:GRID_W - WIN_W + RPB_W] = f["na_rpb"][0]
    arrays["rpb"] = np.broadcast_to(pad.reshape(HEADS, 2, RPB_H, 1, RPB_PITCH), (HEADS, 2, RPB_H, GRID_W, RPB_PITCH))
    arrays["ident_d"] = np.eye(P, dtype=np.float32)
    arrays["ones_d"] = np.ones((P, P), np.float32)
    arrays["pair_ones_d"] = np.kron(np.eye(2), np.ones((DH, DH))).astype(np.float32)
    arrays["iota_d"] = np.ascontiguousarray(np.broadcast_to(np.arange(P, dtype=np.float32), (P, P)))
    arrays["sub_keys"] = f["peer_sub_keys"][0].transpose(2, 0, 1)
    w = by_block(f["w_in"][0], KC)
    order = [b for n in range(HEADS) for b in
             (n, 8 + n, 16 + n, 24 + n, 32 + n, 40 + n, 48 + 2 * n, 49 + 2 * n, 64 + 2 * n, 65 + 2 * n)]
    arrays["w_in"] = chunks(w[order])
    arrays["w_branch"] = np.stack([chunks(by_block(f["w_branch_da"][0], 8)), chunks(by_block(f["w_branch_na"][0], 8))],
                                  axis=1).reshape(2 * KC, P, CH)
    arrays["w_out"] = chunks(by_block(f["w_out"][0], KC))
    arrays["w_query"] = chunks(by_block(f["peer_w_query"][0], KC))
    arrays["peer_u"] = chunks(f["peer_u"][0].reshape(P, P, KC, P).transpose(0, 3, 2, 1))
    arrays["peer_v"] = f["peer_v"][0].reshape(P, P, 2, CH).transpose(0, 2, 1, 3)

    nc = bacc.Bacc("TRN2", target_bir_lowering=False, num_devices=1)
    feeds, args = {}, []
    for name in ("h_turned", "gains", "lambdas", "alibi", "na_mask", "rpb", "ident_d", "ones_d", "pair_ones_d",
                 "iota_d", "sub_keys", "w_in", "w_branch", "w_out", "w_query", "peer_u", "peer_v"):
        a = np.ascontiguousarray(arrays[name])
        feeds[f"in_{name}"] = a
        args.append(nc.dram_tensor(f"in_{name}", a.shape, mybir.dt.from_np(a.dtype), kind="ExternalInput").ap())
    out = nc.dram_tensor("out_h", (T, D), F32, kind="ExternalOutput").ap()
    block_kernel(nc, *args, out)
    r = run_bass_kernel_spmd(nc, [feeds], core_ids=[0])
    return r.results[0]["out_h"][None]
```
